# Optimizing a Trainium2 kernel written in Bass

```python
import jax, jax.numpy as jnp
from jax import lax
import numpy as np

D_MODEL = 2048
BATCH = 1
SEQ = 256
DEPTH = 1

CTX_LEN = 256
GRID_W = 64
MIX_W = 2 * D_MODEL
SSD_W = MIX_W // 2
SSD_HEADS = 32
SSD_HEAD_DIM = SSD_W // SSD_HEADS
SSD_GROUPS = 8
SSD_STATE = 128
SSD_CHUNK = 128
CONV_W = 5
MLP_W = MIX_W - SSD_W
MLP_GROUPS = 16
MLP_GROUP_DIM = MLP_W // MLP_GROUPS
MLP_CHUNK = 128
GN = SSD_GROUPS * SSD_STATE
XBC_W = SSD_W + 2 * GN
DT_W = 2 * SSD_HEADS
IN_W = XBC_W + DT_W + SSD_W + 3 * MLP_W
EPS = 1e-6


def _rmsnorm(x, g):
    xf = x.astype(jnp.float32)
    r = lax.rsqrt(jnp.mean(xf * xf, axis=-1, keepdims=True) + EPS)
    return (xf * r).astype(x.dtype) * g

def _dwconv_rows(x, w, b, n_rows, row_len):
    bsz, L, C = x.shape
    pad = CONV_W // 2
    xp = jnp.pad(x.reshape(bsz, n_rows, row_len, C), ((0, 0), (0, 0), (pad, pad), (0, 0)))
    y = b
    for k in range(CONV_W):
        y = y + xp[:, :, k:k + row_len] * w[k]
    return y.reshape(bsz, L, C)

def _ssd(xh, dt, A, Bm, Cm, h0, with_output):
    f32 = jnp.float32
    bsz, L, H, P = xh.shape
    G, N, Q = SSD_GROUPS, SSD_STATE, SSD_CHUNK
    R = H // G
    nc = L // Q
    x = xh.astype(f32).reshape(bsz, nc, Q, G, R, P)
    dtc = dt.reshape(bsz, nc, Q, G, R)
    a = dtc * A.reshape(G, R)
    xdt = x * dtc[..., None]
    Bc = Bm.astype(f32).reshape(bsz, nc, Q, G, N)
    Cc = Cm.astype(f32).reshape(bsz, nc, Q, G, N)
    acs = jnp.cumsum(a, axis=2)
    a_tot = acs[:, :, -1]
    decay_to_end = jnp.exp(a_tot[:, :, None] - acs)
    states = jnp.einsum('bckgn,bckgr,bckgrp->bcgrpn', Bc, decay_to_end, xdt)

    def step(h, inp):
        s, at = inp
        return h * jnp.exp(at)[..., None, None] + s, h

    hT, h_starts = lax.scan(step, h0.reshape(bsz, G, R, P, N),
                            (jnp.moveaxis(states, 1, 0), jnp.moveaxis(a_tot, 1, 0)))
    final = hT.reshape(bsz, H, P, N)
    if not with_output:
        return None, final
    h_starts = jnp.moveaxis(h_starts, 0, 1)
    CB = jnp.einsum('bcqgn,bckgn->bcgqk', Cc, Bc)
    acs_t = jnp.moveaxis(acs, 2, -1)
    diff = acs_t[..., :, None] - acs_t[..., None, :]
    mask = jnp.tril(jnp.ones((Q, Q), dtype=bool))
    Lmat = jnp.exp(jnp.where(mask, diff, -jnp.inf))
    y_diag = jnp.einsum('bcgqk,bcgrqk,bckgrp->bcqgrp', CB, Lmat, xdt)
    y_off = jnp.einsum('bcqgn,bcgrpn,bcqgr->bcqgrp', Cc, h_starts, jnp.exp(acs))
    return (y_diag + y_off).reshape(bsz, L, H, P), final

def _ssd_prep(z, conv_w, conv_b, dt_bias, a_log, n_rows, row_len):
    bsz, L, _ = z.shape
    xbc = jax.nn.silu(_dwconv_rows(z[..., :XBC_W], conv_w, conv_b, n_rows, row_len))
    xh = xbc[..., :SSD_W].reshape(bsz, L, SSD_HEADS, SSD_HEAD_DIM)
    Bm = xbc[..., SSD_W:SSD_W + GN].reshape(bsz, L, SSD_GROUPS, SSD_STATE)
    Cm = xbc[..., SSD_W + GN:XBC_W].reshape(bsz, L, SSD_GROUPS, SSD_STATE)
    dt_raw = z[..., XBC_W:XBC_W + DT_W].astype(jnp.float32).reshape(bsz, L, 2, SSD_HEADS)
    dt = jax.nn.softplus(dt_raw + dt_bias.astype(jnp.float32))
    A = -jnp.exp(a_log.astype(jnp.float32))
    return xh, Bm, Cm, dt, A

def _ssd_bidir(xh, Bm, Cm, dt, A, h0f, h0b, with_output):
    flip = lambda t: jnp.flip(t, axis=1)
    y_f, h_f = _ssd(xh, dt[:, :, 0], A[0], Bm, Cm, h0f, with_output)
    y_b, h_b = _ssd(flip(xh), flip(dt[:, :, 1]), A[1], flip(Bm), flip(Cm), h0b, with_output)
    if not with_output:
        return None, h_f, h_b
    return y_f + flip(y_b), h_f, h_b

def _mix_out(z, xh, y_ssd, d_skip, g_ssd, g_v, w_s, b_s, g_mlp, w_out):
    bsz, L, _ = z.shape
    o = XBC_W + DT_W
    z_ssd = z[..., o:o + SSD_W]
    u = z[..., o + SSD_W:o + SSD_W + MLP_W]
    v = z[..., o + SSD_W + MLP_W:o + SSD_W + 2 * MLP_W]
    z_mlp = z[..., o + SSD_W + 2 * MLP_W:]
    y = (y_ssd + d_skip.astype(jnp.float32)[:, None] * xh.astype(jnp.float32))
    y = y.reshape(bsz, L, SSD_W).astype(z.dtype)
    y_a = _rmsnorm(y * jax.nn.silu(z_ssd), g_ssd)
    vn = _rmsnorm(v, g_v).reshape(bsz, L // MLP_CHUNK, MLP_CHUNK, MLP_GROUPS, MLP_GROUP_DIM)
    sg = jnp.einsum('gqk,bckgd->bcqgd', w_s, vn) + jnp.swapaxes(b_s, 0, 1)[:, :, None]
    y_b = _rmsnorm(u * sg.reshape(bsz, L, MLP_W) * jax.nn.silu(z_mlp), g_mlp)
    return jnp.concatenate([y_a, y_b], axis=-1) @ w_out

def first_inputs(seed: int = 0) -> dict:
    key = jax.random.key(seed)
    ks = jax.random.split(key, 20)
    D = D_MODEL
    nrm = jax.random.normal
    x = nrm(ks[0], (BATCH, SEQ, D), jnp.float32)
    c = nrm(ks[1], (BATCH, D), jnp.float32)
    ctx = nrm(ks[2], (BATCH, CTX_LEN, D), jnp.float32)
    c_ctx = nrm(ks[3], (D,), jnp.float32)
    w_ada = nrm(ks[4], (DEPTH, D, 3 * D), jnp.float32) * (0.5 * D ** -0.5)
    b_ada = 0.01 * nrm(ks[5], (DEPTH, 3 * D), jnp.float32)
    g_pre = 1.0 + 0.05 * nrm(ks[6], (DEPTH, D), jnp.float32)
    g_post = 1.0 + 0.05 * nrm(ks[7], (DEPTH, D), jnp.float32)
    w_in = nrm(ks[8], (DEPTH, D, IN_W), jnp.float32) * D ** -0.5
    conv_w = nrm(ks[9], (DEPTH, CONV_W, XBC_W), jnp.float32) * CONV_W ** -0.5
    conv_b = 0.01 * nrm(ks[10], (DEPTH, XBC_W), jnp.float32)
    u_dt = jax.random.uniform(ks[11], (DEPTH, 2, SSD_HEADS), jnp.float32)
    dt0 = jnp.exp(u_dt * (np.log(0.1) - np.log(0.001)) + np.log(0.001))
    dt_bias = dt0 + jnp.log(-jnp.expm1(-dt0))
    a_log = jnp.log(jax.random.uniform(ks[12], (DEPTH, 2, SSD_HEADS), jnp.float32, 1.0, 16.0))
    d_skip = 1.0 + 0.1 * nrm(ks[13], (DEPTH, SSD_HEADS), jnp.float32)
    g_ssd = 1.0 + 0.05 * nrm(ks[14], (DEPTH, SSD_W), jnp.float32)
    g_v = 1.0 + 0.05 * nrm(ks[15], (DEPTH, MLP_W), jnp.float32)
    w_s = nrm(ks[16], (DEPTH, MLP_GROUPS, MLP_CHUNK, MLP_CHUNK), jnp.float32) * (0.5 * MLP_CHUNK ** -0.5)
    b_s = 1.0 + 0.05 * nrm(ks[17], (DEPTH, MLP_GROUPS, MLP_CHUNK), jnp.float32)
    g_mlp = 1.0 + 0.05 * nrm(ks[18], (DEPTH, MLP_W), jnp.float32)
    w_out = nrm(ks[19], (DEPTH, MIX_W, D), jnp.float32) * MIX_W ** -0.5
    return {"x": x, "c": c, "ctx": ctx, "c_ctx": c_ctx, "w_ada": w_ada, "b_ada": b_ada,
            "g_pre": g_pre, "g_post": g_post, "w_in": w_in, "conv_w": conv_w, "conv_b": conv_b,
            "dt_bias": dt_bias, "a_log": a_log, "d_skip": d_skip, "g_ssd": g_ssd, "g_v": g_v,
            "w_s": w_s, "b_s": b_s, "g_mlp": g_mlp, "w_out": w_out}

def first_block(x, c, ctx, c_ctx, w_ada, b_ada, g_pre, g_post, w_in, conv_w, conv_b,
              dt_bias, a_log, d_skip, g_ssd, g_v, w_s, b_s, g_mlp, w_out):
    bsz, L, _ = x.shape
    ROWS = L // GRID_W
    sc = jax.nn.silu(c)
    scc = jax.nn.silu(c_ctx)
    h0 = jnp.zeros((bsz, SSD_HEADS, SSD_HEAD_DIM, SSD_STATE), jnp.float32)
    for l in range(DEPTH):
        last = l == DEPTH - 1
        shift, scale, gate = jnp.split(sc @ w_ada[l] + b_ada[l], 3, axis=-1)
        shift_c, scale_c, gate_c = jnp.split(scc @ w_ada[l] + b_ada[l], 3, axis=-1)
        hc = _rmsnorm(ctx, g_pre[l]) * (1.0 + scale_c) + shift_c
        zc = hc @ (w_in[l][:, :XBC_W + DT_W] if last else w_in[l])
        xh_c, B_c, C_c, dt_c, A = _ssd_prep(zc, conv_w[l], conv_b[l], dt_bias[l], a_log[l], 1, CTX_LEN)
        y_c, h_f, h_b = _ssd_bidir(xh_c, B_c, C_c, dt_c, A, h0, h0, not last)
        hx = _rmsnorm(x, g_pre[l]) * (1.0 + scale[:, None]) + shift[:, None]
        zx = hx @ w_in[l]
        xh, Bm, Cm, dt, A = _ssd_prep(zx, conv_w[l], conv_b[l], dt_bias[l], a_log[l], ROWS, GRID_W)
        y_x, _, _ = _ssd_bidir(xh, Bm, Cm, dt, A, h_f, h_b, True)
        out = _rmsnorm(_mix_out(zx, xh, y_x, d_skip[l], g_ssd[l], g_v[l], w_s[l], b_s[l],
                                g_mlp[l], w_out[l]), g_post[l])
        x = x + gate[:, None] * out
        if not last:
            out_c = _rmsnorm(_mix_out(zc, xh_c, y_c, d_skip[l], g_ssd[l], g_v[l], w_s[l], b_s[l],
                                      g_mlp[l], w_out[l]), g_post[l])
            ctx = ctx + gate_c * out_c
    return x


DEPTH_2 = 2

N_EVEN = (DEPTH_2 + 1) // 2
N_ODD = DEPTH_2 // 2

A_HEAD_DIM = 64
A_HEADS = D_MODEL // 128
A_KV_HEADS = A_HEADS // 8
A_WIDTH = A_HEADS * A_HEAD_DIM
A_KV_WIDTH = A_KV_HEADS * A_HEAD_DIM
WINDOW = 128
A_BLOCK = 128
ROPE_THETA = 10000.0

B_HEAD_DIM = 128
B_HEADS = (D_MODEL // 2) // B_HEAD_DIM
B_WIDTH = B_HEADS * B_HEAD_DIM
B_CHUNK = 16
LB_FLOOR = 1e-30

C_HEAD_DIM = 128
C_HEADS = D_MODEL // C_HEAD_DIM
C_WIDTH = C_HEADS * C_HEAD_DIM
C_BLOCK = 128

EVEN_SPLITS = [A_WIDTH, A_KV_WIDTH, A_KV_WIDTH, A_WIDTH, B_WIDTH, B_WIDTH, B_WIDTH, B_WIDTH]
EVEN_IN = sum(EVEN_SPLITS)
EVEN_MIX = A_WIDTH + B_WIDTH
ODD_IN = 4 * C_WIDTH


def rmsnorm(x, w):
    xf = x.astype(jnp.float32)
    return xf * lax.rsqrt(jnp.mean(xf * xf, axis=-1, keepdims=True) + EPS) * w.astype(jnp.float32)

def rope(x, pos):
    half = x.shape[-1] // 2
    inv_freq = 1.0 / (ROPE_THETA ** (jnp.arange(half, dtype=jnp.float32) / half))
    ang = pos[:, None] * inv_freq[None, :]
    cos = jnp.cos(ang)[None, :, None, :]
    sin = jnp.sin(ang)[None, :, None, :]
    x1, x2 = x[..., :half], x[..., half:]
    return jnp.concatenate([x1 * cos - x2 * sin, x2 * cos + x1 * sin], axis=-1)

def sliding_window_attention(q, k, v, sinks):
    b_, s_ = q.shape[:2]
    nb = s_ // A_BLOCK
    g = A_HEADS // A_KV_HEADS
    qb = q.reshape(b_, nb, A_BLOCK, A_KV_HEADS, g, A_HEAD_DIM)

    def band(t):
        t = t.reshape(b_, nb, A_BLOCK, A_KV_HEADS, A_HEAD_DIM)
        prev = jnp.concatenate([jnp.zeros_like(t[:, :1]), t[:, :-1]], axis=1)
        return jnp.concatenate([prev, t], axis=2)

    kb, vb = band(k), band(v)
    scores = jnp.einsum('bnqhgd,bnkhd->bnhgqk', qb, kb) * (A_HEAD_DIM ** -0.5)
    qpos = jnp.arange(nb)[:, None] * A_BLOCK + jnp.arange(A_BLOCK)[None, :]
    kpos = jnp.arange(nb)[:, None] * A_BLOCK - A_BLOCK + jnp.arange(2 * A_BLOCK)[None, :]
    diff = qpos[:, :, None] - kpos[:, None, :]
    valid = (diff >= 0) & (diff < WINDOW) & (kpos[:, None, :] >= 0)
    scores = jnp.where(valid[None, :, None, None], scores, -1e30)
    sink = jnp.broadcast_to(sinks.astype(jnp.float32).reshape(1, 1, A_KV_HEADS, g, 1, 1),
                            scores.shape[:-1] + (1,))
    probs = jax.nn.softmax(jnp.concatenate([scores, sink], axis=-1), axis=-1)[..., :-1]
    out = jnp.einsum('bnhgqk,bnkhd->bnqhgd', probs, vb)
    return out.reshape(b_, s_, A_WIDTH)

def hgrn2_chunkwise(q, logf, k, v):
    b_, s_, h_, kd = q.shape
    vd = v.shape[-1]
    nc = s_ // B_CHUNK

    def chunks(t):
        return t.reshape(b_, nc, B_CHUNK, h_, t.shape[-1]).transpose(0, 3, 1, 2, 4)

    qc, lc, kc, vc = chunks(q), chunks(logf), chunks(k), chunks(v)
    bcum = jnp.cumsum(lc, axis=3)
    causal = jnp.tril(jnp.ones((B_CHUNK, B_CHUNK), dtype=bool))
    pair = jnp.exp(jnp.minimum(bcum[:, :, :, :, None, :] - bcum[:, :, :, None, :, :], 0.0))
    att = jnp.einsum('bhnik,bhnjk,bhnijk->bhnij', qc, kc, pair)
    att = jnp.where(causal, att, 0.0)
    o_intra = jnp.einsum('bhnij,bhnjv->bhniv', att, vc)

    blast = bcum[:, :, :, -1:]
    u = jnp.einsum('bhnjk,bhnjv->bhnkv', kc * jnp.exp(blast - bcum), vc)
    decay = jnp.exp(blast[:, :, :, 0])

    def step(state, inp):
        d, inc = inp
        return d[..., None] * state + inc, state

    s0 = jnp.zeros((b_, h_, kd, vd), jnp.float32)
    _, s_prev = lax.scan(step, s0, (decay.transpose(2, 0, 1, 3), u.transpose(2, 0, 1, 3, 4)))
    s_prev = s_prev.transpose(1, 2, 0, 3, 4)
    o_inter = jnp.einsum('bhnik,bhnkv->bhniv', qc * jnp.exp(bcum), s_prev)
    o = o_intra + o_inter
    return o.transpose(0, 2, 3, 1, 4).reshape(b_, s_, h_, vd)

def stick_breaking_attention(q, k, v):
    b_, h_, s_, d_ = q.shape
    nb = s_ // C_BLOCK
    qb = q.reshape(b_, h_, nb, C_BLOCK, d_).transpose(2, 0, 1, 3, 4)
    kpos = jnp.arange(s_)
    scale = d_ ** -0.5

    def block(args):
        c, qblk = args
        qpos = c * C_BLOCK + jnp.arange(C_BLOCK)
        z = jnp.einsum('bhqd,bhkd->bhqk', qblk, k) * scale
        before = kpos[None, :] < qpos[:, None]
        log1m = jnp.where(before, jax.nn.log_sigmoid(-z), 0.0)
        rc = lax.cumsum(log1m, axis=3, reverse=True)
        rc_excl = jnp.concatenate([rc[..., 1:], jnp.zeros_like(rc[..., :1])], axis=-1)
        w = jnp.where(before, jnp.exp(jax.nn.log_sigmoid(z) + rc_excl), 0.0)
        return jnp.einsum('bhqk,bhkd->bhqd', w, v)

    o = lax.map(block, (jnp.arange(nb), qb))
    return o.transpose(1, 0, 3, 2, 4).reshape(b_, s_, h_ * d_)

def even_layer(x, pos, ln, w_in, qn, kn, sinks, lb, gn, w_out):
    b_, s_, _ = x.shape
    h = rmsnorm(x, ln).astype(x.dtype)
    proj = h @ w_in
    idx = list(np.cumsum(EVEN_SPLITS)[:-1])
    aq, ak, av, ag, bq, bf, bi, bg = jnp.split(proj, idx, axis=-1)

    aq = rope(rmsnorm(aq.reshape(b_, s_, A_HEADS, A_HEAD_DIM), qn), pos)
    ak = rope(rmsnorm(ak.reshape(b_, s_, A_KV_HEADS, A_HEAD_DIM), kn), pos)
    av = av.reshape(b_, s_, A_KV_HEADS, A_HEAD_DIM).astype(jnp.float32)
    ya = sliding_window_attention(aq, ak, av, sinks) * jax.nn.silu(ag.astype(jnp.float32))

    lbf = lb.astype(jnp.float32)
    logf = jnp.logaddexp(jnp.log(jnp.maximum(lbf, LB_FLOOR)),
                         jnp.log1p(-lbf) + jax.nn.log_sigmoid(bf.astype(jnp.float32)))
    kin = -jnp.expm1(logf)
    shp = (b_, s_, B_HEADS, B_HEAD_DIM)
    ob = hgrn2_chunkwise(jax.nn.silu(bq.astype(jnp.float32)).reshape(shp), logf.reshape(shp),
                         kin.reshape(shp), bi.astype(jnp.float32).reshape(shp))
    yb = rmsnorm(ob, gn) * jax.nn.silu(bg.astype(jnp.float32)).reshape(shp)
    yb = yb.reshape(b_, s_, B_WIDTH)

    y = jnp.concatenate([ya, yb], axis=-1).astype(x.dtype) @ w_out
    return x + y

def odd_layer(x, ln, w_in, w_out):
    b_, s_, _ = x.shape
    h = rmsnorm(x, ln).astype(x.dtype)
    cq, ck, cv, cg = jnp.split(h @ w_in, 4, axis=-1)

    def heads(t):
        return t.reshape(b_, s_, C_HEADS, C_HEAD_DIM).transpose(0, 2, 1, 3).astype(jnp.float32)

    oc = stick_breaking_attention(heads(cq), heads(ck), heads(cv))
    y = (oc * jax.nn.silu(cg.astype(jnp.float32))).astype(x.dtype) @ w_out
    return x + y

def second_inputs(seed: int = 0) -> dict:
    key = jax.random.key(seed)
    ks = jax.random.split(key, 12)
    f32 = jnp.float32
    return {
        "x": jax.random.normal(ks[0], (BATCH, SEQ, D_MODEL), f32),
        "ln_even": 1.0 + 0.02 * jax.random.normal(ks[1], (N_EVEN, D_MODEL), f32),
        "w_in_even": jax.random.normal(ks[2], (N_EVEN, D_MODEL, EVEN_IN), f32) * D_MODEL ** -0.5,
        "q_norm_a": 1.0 + 0.02 * jax.random.normal(ks[3], (N_EVEN, A_HEAD_DIM), f32),
        "k_norm_a": 1.0 + 0.02 * jax.random.normal(ks[4], (N_EVEN, A_HEAD_DIM), f32),
        "sinks_a": jax.random.normal(ks[5], (N_EVEN, A_HEADS), f32),
        "lower_bounds": 0.5 * jax.random.normal(ks[6], (N_EVEN, B_WIDTH), f32),
        "g_norm_b": 1.0 + 0.02 * jax.random.normal(ks[7], (N_EVEN, B_HEAD_DIM), f32),
        "w_out_even": jax.random.normal(ks[8], (N_EVEN, EVEN_MIX, D_MODEL), f32) * EVEN_MIX ** -0.5,
        "ln_odd": 1.0 + 0.02 * jax.random.normal(ks[9], (N_ODD, D_MODEL), f32),
        "w_in_odd": jax.random.normal(ks[10], (N_ODD, D_MODEL, ODD_IN), f32) * D_MODEL ** -0.5,
        "w_out_odd": jax.random.normal(ks[11], (N_ODD, C_WIDTH, D_MODEL), f32) * C_WIDTH ** -0.5,
    }

def second_block(x, ln_even, w_in_even, q_norm_a, k_norm_a, sinks_a, lower_bounds, g_norm_b,
              w_out_even, ln_odd, w_in_odd, w_out_odd):
    pos = jnp.arange(x.shape[1], dtype=jnp.float32)
    lbs = jax.nn.softmax(lower_bounds.astype(jnp.float32), axis=0)
    lbs = jnp.cumsum(lbs, axis=0) - lbs[0]
    for layer in range(DEPTH_2):
        if layer % 2 == 0:
            e = layer // 2
            x = even_layer(x, pos, ln_even[e], w_in_even[e], q_norm_a[e], k_norm_a[e], sinks_a[e],
                           lbs[e], g_norm_b[e], w_out_even[e])
        else:
            o = layer // 2
            x = odd_layer(x, ln_odd[o], w_in_odd[o], w_out_odd[o])
    return x


def setup_inputs(seed=0):
    out = dict(first_inputs(seed))
    for name, value in second_inputs(seed + 1).items():
        if name != "x":
            out[name + "_2"] = value
    return out


def reference(
    x, c, ctx, c_ctx, w_ada, b_ada, g_pre, g_post, w_in, conv_w, conv_b, dt_bias, a_log, d_skip,
    g_ssd, g_v, w_s, b_s, g_mlp, w_out, ln_even_2, w_in_even_2, q_norm_a_2, k_norm_a_2,
    sinks_a_2, lower_bounds_2, g_norm_b_2, w_out_even_2, ln_odd_2, w_in_odd_2, w_out_odd_2,
):
    x = first_block(
        x, c, ctx, c_ctx, w_ada, b_ada, g_pre, g_post, w_in, conv_w, conv_b, dt_bias, a_log,
        d_skip, g_ssd, g_v, w_s, b_s, g_mlp, w_out,
    )
    return second_block(
        x, ln_even_2, w_in_even_2, q_norm_a_2, k_norm_a_2, sinks_a_2, lower_bounds_2,
        g_norm_b_2, w_out_even_2, ln_odd_2, w_in_odd_2, w_out_odd_2,
    )


_drawn_inputs = setup_inputs


def setup_inputs(seed=0):
    import zlib

    import numpy as np

    out = dict(_drawn_inputs(seed))
    spreads = {}
    factors = {'ctx': 4.622,
     'c_ctx': 4.426,
     'b_ada': 4.169,
     'g_post': 3.173,
     'conv_b': 8.0,
     'd_skip': 5.058,
     'g_ssd': 4.526,
     'g_v': 8.0,
     'b_s': 5.33,
     'g_mlp': 4.696,
     'ln_even_2': 4.652,
     'q_norm_a_2': 8.0,
     'k_norm_a_2': 8.0,
     'sinks_a_2': 7.825,
     'g_norm_b_2': 7.903,
     'ln_odd_2': 5.619}
    for name, (base, spread) in spreads.items():
        noise = np.random.default_rng([zlib.crc32(name.encode()), seed]).standard_normal(out[name].shape)
        drawn = base * np.exp(spread * noise) if base else spread * noise
        out[name] = __import__('jax').numpy.asarray(drawn.astype(out[name].dtype))
    for name, factor in factors.items():
        out[name] = (out[name] * factor).astype(out[name].dtype)
    return out
```

```python
import numpy as np
import concourse.bass as bass
from concourse import mybir
from contextlib import ExitStack

F32 = mybir.dt.float32
F32R = mybir.dt.float32r
ALU = mybir.AluOpType
ACT = mybir.ActivationFunctionType
AX = mybir.AxisListType

P = 128
D = 2048
KT = D // P
SEQ = 256
NT = SEQ // P
EPS = 1e-6
NCOL = 512
UPC = 8
GPC = 4

GRID_W, ROWS = 64, 4
SSD_W, HEADS, HD, GROUPS, STATE = 2048, 32, 64, 8, 128
RH = HEADS // GROUPS
GN = GROUPS * STATE
XBC_W = SSD_W + 2 * GN
DT_W = 2 * HEADS
MLP_G = 16
IN_W = XBC_W + DT_W + 4 * SSD_W
TAPS = 5
NBLK = XBC_W // P
ZX = ROWS * (GRID_W + 4)
ZC = SEQ + 4
ZW = ZX + ZC
CW = ZW - 4

A_H, A_D, A_KV = 16, 64, 2
EVEN_W = 6400
B_H, B_D = 8, 128
C_H, C_D = 16, 128
LB_FLOOR = 1e-30

VEC_TILES = [
    [("c", 16), ("c_ctx", 16), ("g_pre", 16), ("g_ssd", 16), ("g_mlp", 16), ("ln_even_2", 16), ("ln_odd_2", 16), ("b_s", 16)],
    [("b_ada", 48), ("conv_b", 32), ("lower_bounds_2", 8), ("g_post", 16)],
    [("conv_w0", 128)],
    [("conv_w1", 32)],
]
VEC = {}
for _t, _rows in enumerate(VEC_TILES):
    _r = 0
    for _n, _k in _rows:
        VEC[_n] = (_t, _r, _k)
        _r += _k
VEC_ROWS = [sum(k for _, k in rows) for rows in VEC_TILES]

CONST = [("ident", 128), ("le", 128), ("lt", 128), ("ge", 128), ("gt", 128), ("one", 128),
         ("neg_f", 128), ("neg_b", 128), ("cos", 64), ("sin", 64), ("band0", 128), ("band1", 128)]
CAT, _o = {}, 0
for _n, _k in CONST:
    CAT[_n] = _o
    _o += _k
NCONST = _o
LEVELS = 7


def constants():
    i = np.arange(P)
    t, q = i[:, None], i[None, :]
    f = np.float32
    inv = (1.0 / (10000.0 ** (np.arange(32, dtype=f) / f(32)))).astype(f)
    ang = (np.arange(SEQ, dtype=f)[:, None] * inv[None, :]).astype(f)
    rope = lambda fn: fn(ang).astype(f).reshape(NT, P, 32).transpose(1, 0, 2).reshape(P, 64)
    parts = {
        "ident": t == q, "le": t <= q, "lt": t < q, "ge": t >= q, "gt": t > q, "one": t + q >= 0,
        "neg_f": np.where(t > q, -1e30, 0), "neg_b": np.where(t < q, -1e30, 0),
        "cos": rope(np.cos), "sin": rope(np.sin),
        "band0": np.where(q <= t, 0, -1e30), "band1": np.where(q > t, 0, -1e30),
    }
    base = np.concatenate([np.asarray(parts[n]).astype(f) for n, _ in CONST], 1)
    lev = [(t == q)]
    for l in range(1, LEVELS + 1):
        s = 2 ** l
        lev.append((t // s == q // s) & (t % s < s // 2) & (q % s >= s // 2))
    return base, np.stack(lev, 1).astype(f).reshape(P, 8 * P)

PHASES = [
    ("B0", 1, "wide", 512), ("DT", 1, "dt", 64), ("B1", 1, "wide", 512), ("X", 4, "wide", 512), ("C", 2, "feat", 512),
    ("V", 4, "tok", 512), ("U", 4, "tok", 512), ("M", 4, "tok", 512), ("S", 4, "tok", 512),
    ("O1", 8, "tok2", 512),
    ("BF0", 1, "feat", 512), ("BQ0", 1, "feat", 512), ("BF1", 1, "feat", 512), ("BQ1", 1, "feat", 512),
    ("AK", 1, "tok", 256), ("AQ", 2, "tok", 512), ("BI", 2, "tok", 512), ("BG", 2, "tok", 512), ("AG", 2, "tok", 512),
    ("O2", 4, "tok", 512),
    ("CQ0", 1, "feat", 512), ("CK0", 1, "feat", 512), ("CV0", 1, "tok", 512),
    ("CR", 9, "quad", 512), ("CG", 4, "tok", 512), ("O3", 4, "tok", 512),
]

PAIR0 = {"BQ0": 1, "BQ1": 1, "AQ": 1, "BI": 1, "BG": 1, "AG": 1, "O2": 1, "CQ0": 1, "CV0": 1, "CG": 1, "O3": 1}


def pair_of(ph, j):
    return (j + PAIR0.get(ph, 0)) % 2


def banks_of(ph, mode, j):
    if mode == "wide":
        return [0, 1, 2, 3]
    if mode == "dt":
        return [0]
    if mode == "tok2":
        return [] if j % 2 == 0 else [2 * (j // 2 % 2), 2 * (j // 2 % 2) + 1]
    return [2 * pair_of(ph, j), 2 * pair_of(ph, j) + 1]


LEV0, LEV1 = 18, 36
HEAD_BEAT = 66
HGRN_BEAT = 73
TURN_BEAT = (93, 95, 97, 99, 101, 103, 105, 106)
_users = sorted([(HEAD_BEAT + 2 * h, "scores", h) for h in range(A_H)] + [(HGRN_BEAT + 2 * g, "hgrn", g) for g in range(4)]
                + [(b, "turn", x) for x, b in enumerate(TURN_BEAT)])
SIDE_USER = {(kind, x): n for n, (_, kind, x) in enumerate(_users)}

STICK_BEAT = 24
TURN3_BEAT = (104, 106, 112, 116, 122, 124, 128, 129)
_users = sorted([(STICK_BEAT + 6 * h + 6, "out", h) for h in range(C_H)] + [(b, "turn", x) for x, b in enumerate(TURN3_BEAT)])
SIDE3_USER = {(kind, x): n for n, (_, kind, x) in enumerate(_users)}


def level(a, l, up):
    s = 2 ** (l - 1)
    return a.rearrange("p h (n s) -> p (h n) s", s=2 * s)[:, :, up * s:(up + 1) * s]



def two_blocks_kernel(nc, ins, out):
    chunk0, c = {}, 0
    before = {}
    uses = [0] * 4
    for name, n, mode, _ in PHASES:
        chunk0[name] = c
        for j in range(n):
            before[name, j] = list(uses)
            for b in banks_of(name, mode, j):
                uses[b] += 1
        c += n
    mode_of = {name: mode for name, _, mode, _ in PHASES}
    ncol_of = {name: ncol for name, _, _, ncol in PHASES}
    names = [name for name, *_ in PHASES]
    count_of = {name: n for name, n, _, _ in PHASES}

    def next_ncol(name, j):
        if j + 1 < count_of[name]:
            return ncol_of[name]
        k = names.index(name) + 1
        return ncol_of[names[k]] if k < len(names) else None

    base = nc.sbuf_base
    base = (base + 31) // 32 * 32
    placed = []

    def at(name, kb, shape, dt=F32):
        t = nc.alloc_sbuf_tensor_at(name, shape, dt, offset=base + int(kb * 1024))
        placed.append((name, kb, int(np.prod(shape[1:])) * 4 / 1024))
        return t

    RAW = at("raw", 0, [P, 4, 2, NCOL])
    WHI = at("w_hi", 16, [P, 4, 2, NCOL], F32R)
    WLO = at("w_lo", 32, [P, 4, 2, NCOL], F32R)
    HHI = at("h_hi", 48, [P, 2, KT, SEQ], F32R)
    HLO = at("h_lo", 80, [P, 2, KT, SEQ], F32R)
    ADA = at("ada_ring", 48, [P, 8, 4, NCOL])
    kb = 192
    CON = at("con", kb, [P, NCONST]); kb += NCONST * 4 / 1024
    VT = at("vec_t", kb, [P, 4, P]); kb += 2
    BCS = at("bc_small", kb, [P, 160]); kb += 0.625
    IDR = at("ident_r", kb, [P, P], F32R); kb += 0.5
    NEGR = at("neg_r", kb, [P, 2, P], F32R); kb += 1
    MOD = at("mod", kb, [P, 6, KT]); kb += 0.375
    ADAV = at("ada_v", kb, [P, 48, 2]); kb += 0.375
    STAT = at("stat", kb, [P, 64]); kb += 0.25
    DTV = at("dt", kb, [P, 4, 64]); kb += 1
    ACS = at("acs", kb, [P, 3, NT, 64]); kb += 1.5
    WCX = at("w_ctx", kb, [P, NT, 64]); kb += 0.5
    ART = at("acs_rows", kb, [64, 2, SEQ], F32R); kb += 2
    assert kb * 1024 + base <= nc.sbuf_usable_end, kb
    con = lambda n, r=P: CON[0:r, CAT[n]:CAT[n] + dict(CONST)[n]]
    vec = lambda n, k, w=1: VT[:, VEC[n][0], VEC[n][1] + k:VEC[n][1] + k + w]
    XIN = at("x_in", 128, [P, 2, NT, D])
    JUNK = at("junk", 112, [P, D])
    ADR = at("ada_rows", 160, [2, 3 * D])
    VR = at("vec_rows", 184, [P, 4, P])
    HF = at("h_f", 186, [P, 2, 2 * SEQ])
    BT = at("bT", 112, [P, GROUPS, SEQ])
    CT = at("cT", 120, [P, GROUPS, SEQ])
    XW = at("x_w", 120, [P, 2, NT, 512])
    XH = at("x_h", 128, [P, NT, SSD_W])
    ST = at("states", 144, [P, 2, SSD_W])
    BK = at("b_ctx", 160, [P, NT, GN])
    ZB = at("z_blk", 168, [P, 4, 512])
    CV = at("conv", 176, [P, 4, 512])
    XC = at("x_ctx", 184, [P, NT, 512])
    BG = at("b_grp", 188, [P, NT, 2, P])
    AW = at("dt_tmp", 120, [P, 4, 4, 64])
    DTC = at("dt_cols", 124, [64, 2 * SEQ])

    V = at("v", 64, [P, NT, D])
    T = at("t", 96, [P, NT, D])
    WS = at("w_s_rows", 160, [P, MLP_G, P])
    WST = at("w_sT", 176, [P, MLP_G, P])
    GV = at("g_v_bc", 184, [P, D])
    Y = at("y", 64, [P, NT, D])
    GB = at("grp_bc", 168, [P, 2, SEQ])
    CBS = at("cb", 170, [P, NT, SEQ])
    SEL = at("sel", 172, [64, 2, RH], F32R)
    EX = at("ex", 172.5, [P, 2, 768])
    MM = at("m", 178.5, [P, 2, NT, SEQ])
    YT = at("y_tmp", 182.5, [P, NT, 256])
    SG = at("gate_tmp", 184.5, [P, NT, NCOL])
    GHI = at("g_hi", 112, [P, KT, SEQ], F32R)
    GLO = at("g_lo", 128, [P, KT, SEQ], F32R)
    X1 = at("x1", 144, [P, NT, D])
    O = at("o", 64, [P, NT, D])
    XR = at("x_again", 96, [P, NT, D])
    GG = at("gate_bc", 160, [P, D])
    DUMP = at("dump", 188.5, [P, NCOL])

    kb2 = 192 + (NCONST * 4 / 1024) + 2 + 0.625 + 0.5 + 1 + 0.375 * 2 + 0.25
    NB = at("norm_bc", kb2, [P, 144])
    GNC = at("g_norm_b_col", kb2 + 0.5625, [P, 1])
    LBC = at("lb", kb2 + 0.625, [P, 6, B_H])
    ST2 = at("stat2", kb2 + 0.8125, [P, 2, NT, 18])
    STB = at("stat_b", kb2 + 1.125, [P, 2, NT, B_H])
    SMX = at("soft", kb2 + 1.25, [P, 2, 6, NT])
    ST3 = at("stat3", kb2 + 1.375, [P, 16])
    XN = at("x_n", 64, [P, NT, D])
    AQ = at("aq", 64, [P, NT, 18 * A_D])
    ATT = at("att", 96, [P, 2, 4, NT, P])
    AT8 = at("att8", 104, [P, 2, 4, P])
    U_ = at("log_f", 112, [P, 2, 4, SEQ])
    VV = at("suffix", 120, [P, 2, 4, SEQ])
    BQ_ = at("bq", 128, [P, 2, 4, SEQ])
    KI = at("k_in", 136, [P, 2, 4, SEQ])
    QT = at("aqT", 112, [A_D, 16, SEQ])
    BI_ = at("bi", 128, [P, NT, B_H * B_D])
    YA = at("ya", 160, [P, NT, A_H * A_D])
    AV = at("av", 168, [P, NT, P])
    KTT = at("akT", 169, [A_D, 2, SEQ])
    PA = at("p_a", 171, [P, 2, 384])
    RT = at("rope_tmp", 174, [P, 4, 18 * 32])
    SQ = at("sq", 174, [P, NT, 18 * A_D])
    WL = at("w_lev", 176, [P, 2, 4, SEQ])
    PT = at("p_aT", 174, [P, 2, 3, P])
    OB = at("ob", 177, [P, NT, B_H * B_D])
    SG2 = at("gate2", 185, [P, NT, NCOL])
    P1 = at("bf_raw", 184, [P, 4, SEQ])
    HM = at("level_masks", 188, [P, 8, P])

    TA = at("soft_tmp", 64, [P, 2, 384])
    SPM = at("softplus", 67, [P, 2, 3, P])
    W3 = at("w_stick", 70, [P, 2, 3, P])
    NEG3 = at("neg_ones", 73, [P, 2, P])
    NM3 = at("neg_mask", 74, [P, P], F32R)
    OC = at("oc", 96, [P, NT, D])
    QF = at("cq", 160, [P, 2, 4, SEQ])
    KF = at("ck", 168, [P, 2, 4, SEQ])
    VF = at("cv", 176, [P, 2, NT, NCOL])
    SG3 = at("gate3", 184, [P, NT, NCOL])

    ACC = [nc.alloc_psum_tensor(f"acc{b}", [P, 512], F32) for b in range(4)]
    SB = [nc.alloc_psum_tensor(f"side{b}", [P, 512], F32) for b in range(4)]

    ctx = ExitStack()
    with ctx:
        def sem(name):
            return ctx.enter_context(nc.semaphore(name))

        con_in, vec_in, x_in, bc_in = sem("con_in"), sem("vec_in"), sem("x_in"), sem("bc_in")
        ada_in = [sem(f"ada_in{s}") for s in range(8)]
        ada_used = sem("ada_used")
        raw_in = [sem(f"raw_in{s}") for s in range(4)]
        hi_ready, lo_ready, unit_used = sem("hi_ready"), sem("lo_ready"), sem("unit_used")
        acc_done = [sem(f"acc_done{b}") for b in range(4)]
        acc_free = [sem(f"acc_free{b}") for b in range(4)]
        vec_turned, vec_ok, ada_done, ada_ok, mod_ok = sem("vec_turned"), sem("vec_ok"), sem("ada_done"), sem("ada_ok"), sem("mod_ok")
        ssq_ok, std_ok, xn_ok = sem("ssq_ok"), sem("std_ok"), sem("xn_ok")
        turned, hf_ok, h_ok = sem("turned"), sem("hf_ok"), sem("h_ok")
        r_const = sem("r_const")
        act_seq, dve_seq, pool_step = sem("act_seq"), sem("dve_seq"), sem("pool_step")
        dtc_ok, dt_turned = sem("dtc_ok"), sem("dt_turned")
        z_ok, conv_ok, silu_ok, t_done, t_free = sem("z_ok"), sem("conv_ok"), sem("silu_ok"), sem("t_done"), sem("t_free")
        dtr_ok, dte_ok, dtl_ok, a_ok, cums_done, cums_ok = sem("dtr_ok"), sem("dte_ok"), sem("dtl_ok"), sem("a_ok"), sem("cums_done"), sem("cums_ok")
        xw_ok, st_done, st_free, bg_ok = sem("xw_ok"), sem("st_done"), sem("st_free"), sem("bg_ok")
        ws_in, gv_in, xr_in = sem("ws_in"), sem("gv_in"), sem("xr_in")
        ws_turned, ws_ok, v_ok, vstd_ok, vn_ok, sg_done, sg_ok = (sem(n) for n in (
            "ws_turned", "ws_ok", "v_ok", "vstd_ok", "vn_ok", "sg_done", "sg_ok"))
        gb_ok, yd_ok, cb_done, cbs_ok, yo_done, yo_used, r_done, e_ok, m_ok, y_done, y_ok = (sem(n) for n in (
            "gb_ok", "yd_ok", "cb_done", "cbs_ok", "yo_done", "yo_used", "r_done", "e_ok", "m_ok", "y_done", "y_ok"))
        t_ok, gate_ok, gate_free, tsq_ok, tstd_ok, tn_ok, h_turned, h_hi, h_lo = (sem(n) for n in (
            "t_ok", "gate_ok", "gate_free", "tsq_ok", "tstd_ok", "tn_ok", "h_turned", "h_hi", "h_lo"))
        yg_ok, ysq_ok, ystd_ok, yn_ok = (sem(n) for n in (
            "yg_ok", "ysq_ok", "ystd_ok", "yn_ok"))
        gg_done, gg_ok, osq_ok, o_ok, ostd_ok, x_ok = (sem(n) for n in (
            "gg_done", "gg_ok", "osq_ok", "o_ok", "ostd_ok", "x_ok"))
        nsq_ok, nrt_ok, nxn_ok = sem("norm_squares_ok"), sem("norm_root_ok"), sem("norm_ok")
        nb_in, hm_in, lb_sem, p1_ok, sp_ok, la_ok, lx_ok, logf_ok, ki_ok, bq_ok = (sem(n) for n in (
            "nb_in", "hm_in", "lb_sem", "p1_ok", "sp_ok", "la_ok", "lx_ok", "logf_ok", "ki_ok", "bq_ok"))
        we_ok, wl_ok, uv_ok, at_done, at_ok, bi_ok = (sem(n) for n in (
            "we_ok", "wl_ok", "uv_ok", "at_done", "at_ok", "bi_ok"))
        aq_ok, asq_ok, arms_ok, rope_ok, aq_turned, qt_ok = (sem(n) for n in (
            "aq_ok", "asq_ok", "arms_ok", "rope_ok", "aq_turned", "qt_ok"))
        sc_done, side_free, ms_ok, pe_ok, pt_done, pt_ok, pv_done, ya_ok = (sem(n) for n in (
            "sc_done", "side_free", "ms_ok", "p_exp_ok", "pt_done", "pt_ok", "pv_done", "ya_ok"))
        ob_done, obc_ok, obr_ok, y2_turned, y2_hi, yb_ok = (sem(n) for n in (
            "ob_done", "obc_ok", "obr_ok", "y2_turned", "y2_hi", "yb_ok"))
        y2_lo, aw_ok = sem("y2_lo"), sem("aw_ok")
        qk_ok, cv_ok, n3_ok, z_done, ab_ok, spm_ok, sum_done, w3_ok, oc_done, oc_ok = (sem(n) for n in (
            "qk_ok", "cv_ok", "n3_ok", "z_done", "ab_ok", "spm_ok", "sum_done", "w3_ok", "oc_done", "oc_ok"))
        stored = sem("stored")
        block = ctx.enter_context(nc.Block())

        class Seq:

            def __init__(self, eng, s):
                self.eng, self.s, self.n, self.loop = eng, s, 0, None

            def __call__(self, ins):
                self.n += 1
                ins.then_inc(self.s, 1)
                at_ = self.n if self.loop is None else self.n + self.loop[0] * self.loop[1]
                self.eng.wait_ge(self.s, at_)

            def enter(self, i, per):
                self.loop, self.at = (i, per), self.n

            def leave(self, times):
                i, per = self.loop
                assert self.n - self.at == per, f"{self.n - self.at} steps in the body"
                self.n, self.loop = self.at + per * times, None

        dram = {n: ins[n] for n in ins}
        w_of = {
            "w_in": dram["w_in"][0], "w_out": dram["w_out"][0], "w_in_even_2": dram["w_in_even_2"][0],
            "w_out_even_2": dram["w_out_even_2"][0], "w_in_odd_2": dram["w_in_odd_2"][0],
            "w_out_odd_2": dram["w_out_odd_2"][0], "w_ada": dram["w_ada"][0],
        }
        w_of = {n: w.rearrange("(t p) n -> p t n", p=P) for n, w in w_of.items()}

        def split_steps(eng, one, ph, c, j, mid, evict, last=False, before_evict=3):
            n, nn = ncol_of[ph], next_ncol(ph, j)
            for u in range(3, UPC):
                one(c, u, n)
                if u in mid:
                    mid[u]()
            for u in range(before_evict):
                if not last:
                    one(c + 1, u, nn)
                if UPC + u in mid:
                    mid[UPC + u]()
            evict()

        @block.sync
        def _(sp):
            sp.dma_start(CON[:], dram["const_a"]).then_inc(con_in, 16)
            for t, rows in enumerate(VEC_TILES):
                for n, k in rows:
                    if n.startswith("conv_w"):
                        src = dram["conv_w"][0].rearrange("k (b p) -> (k b) p", p=P)
                        src = src[0:128] if n == "conv_w0" else src[128:160]
                    else:
                        a = dram[n]
                        while len(a.shape) > 1 and a.shape[0] == 1:
                            a = a[0]
                        src = a if len(a.shape) == 2 else a.rearrange("(r p) -> r p", p=P)
                    r0 = VEC[n][1]
                    sp.dma_start(VR[r0:r0 + k, t, :], src).then_inc(vec_in, 16)
            sp.dma_start(BCS[:, 0:64], dram["dt_bias"].rearrange("o d h -> (o d h)").partition_broadcast(P)).then_inc(bc_in, 16)
            sp.dma_start(BCS[:, 64:128], dram["a_log"].rearrange("o d h -> (o d h)").partition_broadcast(P)).then_inc(bc_in, 16)
            sp.dma_start(BCS[:, 128:160], dram["d_skip"][0].partition_broadcast(P)).then_inc(bc_in, 16)

            def ada(g, s, wait):
                if wait:
                    sp.wait_ge(ada_used, g - 7)
                sp.dma_start(ADA[:, s], w_of["w_ada"][:, 4 * (s % 4):4 * (s % 4) + 4,
                                                      bass.ds((g - s % 4) * 128, NCOL)]).then_inc(ada_in[s], 16)

            for s in range(4):
                ada(s, s, False)
            for s, n in enumerate(("x", "ctx")):
                sp.dma_start(XIN[:, s], dram[n][0].rearrange("(t p) d -> p t d", p=P)).then_inc(x_in, 16)
            for s in range(4, 8):
                ada(s, s, False)
            with sp.Fori(1, 6) as i:
                for s in range(8):
                    ada(i * 8 + s, s, True)

            def load(ph, c, j, src, col, n, kt0=0, wait=True):
                if not isinstance(c, int):
                    col = sp.snap(col)
                for u in range(UPC):
                    if wait or u >= 4:
                        sp.wait_ge(lo_ready, c * UPC + u - 3)
                    k = (kt0 + 2 * u) % (w_of[src].shape[1])
                    sp.dma_start(RAW[:, u % 4, :, 0:n],
                                 w_of[src][:, k:k + 2, bass.ds(col, n)]).then_inc(raw_in[u % 4], 16)

            def run(ph, src, col, n=NCOL, count=None):
                cnt = count_of[ph] if count is None else count
                if cnt <= 2:
                    for j in range(cnt):
                        load(ph, chunk0[ph] + j, j, src, col + j * NCOL, n, wait=chunk0[ph] + j > 0)
                else:
                    with sp.Fori(0, cnt) as j:
                        load(ph, j + chunk0[ph], j, src, j * NCOL + col, n)

            run("B0", "w_in", SSD_W)
            run("DT", "w_in", XBC_W, 64)
            run("B1", "w_in", SSD_W + NCOL)
            run("X", "w_in", 0)
            run("C", "w_in", SSD_W + GN)
            off = XBC_W + DT_W
            cV = chunk0["V"]
            load("V", cV, 0, "w_in", off + 2 * D, NCOL)
            sp.wait_ge(bg_ok, 4)
            sp.dma_start(WS[:], dram["w_s"][0].rearrange("g q k -> q g k")).then_inc(ws_in, 16)
            sp.wait_ge(st_done, 8)
            sp.dma_start(GV[:], dram["g_v"][0].partition_broadcast(P)).then_inc(gv_in, 16)
            with sp.Fori(1, 4) as j:
                load("V", j + cV, j, "w_in", j * NCOL + (off + 2 * D), NCOL)
            run("U", "w_in", off + D)
            run("M", "w_in", off + 3 * D)
            run("S", "w_in", off)
            cO = chunk0["O1"]
            load("O1", cO, 0, "w_out", 0, NCOL, kt0=KT)
            load("O1", cO + 1, 0, "w_out", 0, NCOL)
            sp.wait_ge(h_turned, 8)
            sp.dma_start(XR[:], dram["x"][0].rearrange("(t p) d -> p t d", p=P)).then_inc(xr_in, 16)
            for r in range(1, 4):
                load("O1", cO + 2 * r, 0, "w_out", r * NCOL, NCOL, kt0=KT)
                load("O1", cO + 2 * r + 1, 0, "w_out", r * NCOL, NCOL)
            load("BF0", chunk0["BF0"], 0, "w_in_even_2", 3328, NCOL)
            for name, at_, n in (("q_norm_a_2", 0, 64), ("k_norm_a_2", 64, 64), ("sinks_a_2", 128, 16)):
                sp.dma_start(NB[:, at_:at_ + n], dram[name][0].partition_broadcast(P)).then_inc(nb_in, 16)
            sp.dma_start(GNC[:], dram["g_norm_b_2"].rearrange("o p -> p o")).then_inc(nb_in, 16)
            sp.wait_ge(x_ok, 2)
            sp.dma_start(HM[:], dram["const_b"].rearrange("p (l q) -> p l q", l=8)).then_inc(hm_in, 16)
            for ph, col in (("BQ0", 2304), ("BF1", 3328 + NCOL), ("BQ1", 2304 + NCOL)):
                load(ph, chunk0[ph], 0, "w_in_even_2", col, NCOL)
            run("AK", "w_in_even_2", 1024, 256)
            run("AQ", "w_in_even_2", 0)
            run("BI", "w_in_even_2", 4352)
            run("BG", "w_in_even_2", 5376)
            run("AG", "w_in_even_2", 1280)
            for j in range(4):
                load("O2", j + chunk0["O2"], 0, "w_out_even_2", j * NCOL, NCOL, kt0=8)
            C3 = chunk0["CQ0"]
            for q in range(4):
                for x in range(3):
                    load("CR", C3 + 3 * q + x, 0, "w_in_odd_2", x * D + q * NCOL, NCOL)
            run("CG", "w_in_odd_2", 3 * D)
            run("O3", "w_out_odd_2", 0)
            for j in range(4):
                sp.wait_ge(x_ok, 10 + 2 * j + 2)
                sp.dma_start(out[0].rearrange("(t p) d -> p t d", p=P)[:, :, j * NCOL:(j + 1) * NCOL],
                             X1[:, :, j * NCOL:(j + 1) * NCOL]).then_inc(stored, 16)
            sp.wait_ge(stored, 64)

        @block.tensor
        def _(pe):
            def passes(l, r):
                return ((l[0], r[0]), (l[0], r[1]), (l[1], r[0]))

            def unit(ph, c, u, pair, first, last, kt0=0, mode=None, turn=0):
                mode, n = mode_of[ph] if mode is None else mode, ncol_of[ph]
                pe.wait_ge(lo_ready, c * UPC + u + 1)
                s = u % 4
                done = []
                if mode == "wide":
                    for b in range(4):
                        for kk in range(2):
                            kt = 2 * u + kk
                            w = (WHI[:, s, kk, b * P:(b + 1) * P], WLO[:, s, kk, b * P:(b + 1) * P])
                            h = (HHI[:, :, kt, :], HLO[:, :, kt, :])
                            for m, (l, r) in enumerate(passes(w, h)):
                                o = nc.tensor.matmul(ACC[b][:].rearrange("p (a t) -> p a t", a=2), l, r,
                                                     start=first and kk == 0 and m == 0, stop=last and kk == 1 and m == 2)
                        done.append((b, o))
                elif mode == "feat":
                    for b4 in range(4):
                        b = 2 * pair + b4 // 2
                        for kk in range(2):
                            kt = 2 * u + kk
                            w = (WHI[:, s, kk, b4 * P:(b4 + 1) * P], WLO[:, s, kk, b4 * P:(b4 + 1) * P])
                            h = (HHI[:, 0, kt, :], HLO[:, 0, kt, :])
                            for m, (l, r) in enumerate(passes(w, h)):
                                o = nc.tensor.matmul(ACC[b][:, (b4 % 2) * SEQ:(b4 % 2 + 1) * SEQ], l, r,
                                                     start=first and kk == 0 and m == 0 and b4 % 2 == 0,
                                                     stop=last and kk == 1 and m == 2, skip_group_check=True)
                        if b4 % 2:
                            done.append((b, o))
                elif mode == "dt":
                    for kk in range(2):
                        kt = 2 * u + kk
                        w = (WHI[:, s, kk, 0:n], WLO[:, s, kk, 0:n])
                        for m, (l, r) in enumerate(passes(w, (HHI[:, :, kt, :], HLO[:, :, kt, :]))):
                            o = nc.tensor.matmul(ACC[0][0:n, :].rearrange("p (a t) -> p a t", a=2), l, r,
                                                 start=first and kk == 0 and m == 0, stop=last and kk == 1 and m == 2)
                    done.append((0, o))
                else:
                    for t in range(NT):
                        b = 2 * pair + t
                        for kk in range(2):
                            kt = (2 * u + kk + turn) % KT
                            h = tuple(H[:, kt, t * P:(t + 1) * P] for H in left(kt0))
                            w = (WHI[:, s, kk, 0:n], WLO[:, s, kk, 0:n])
                            for m, (l, r) in enumerate(passes(h, w)):
                                o = nc.tensor.matmul(ACC[b][:, 0:n], l, r, start=first and kk == 0 and m == 0,
                                                     stop=last and kk == 1 and m == 2)
                        done.append((b, o))
                if last:
                    for b, o in done[:-1]:
                        o.then_inc(acc_done[b], 1)
                return done

            def left(kt0):
                return {0: (HHI[:, 0], HLO[:, 0]), KT: (GHI, GLO), 1: (HHI[:, 1], HLO[:, 1])}[kt0]

            def chunk(ph, c, j, i=0, hooks={}, kt0=0, first=True, last=True, pair=None, mode=None, turn=0, ahead={}):
                mode = mode_of[ph] if mode is None else mode
                pair = pair_of(ph, j) if pair is None else pair
                for u in range(UPC):
                    if u == 0 and first:
                        for b in banks_of(ph, mode_of[ph], j + 1 if mode == "tok2" else j):
                            n = before[ph, j][b]
                            if n or not isinstance(i, int):
                                pe.wait_ge(acc_free[b], i + n)
                    lastu = last and u == UPC - 1
                    if u in ahead:
                        ahead[u]()
                    done = unit(ph, c, u, pair, first and u == 0, lastu, kt0, mode, turn)
                    if lastu:
                        done[-1][1].then_inc(acc_done[done[-1][0]], 1)
                        pe.wait_ge(acc_done[done[-1][0]], before[ph, j][done[-1][0]] + 1 + i)
                        pe.sem_inc(unit_used, 1)
                    else:
                        done[-1][1].then_inc(unit_used, 1)
                    if u in hooks:
                        hooks[u]()

            pe.wait_ge(con_in, 16)
            pe.wait_ge(vec_in, 16 * 14)
            for t, r in enumerate(VEC_ROWS):
                nc.tensor.transpose(SB[0][:, t * P:t * P + r], VR[0:r, t, :], con("ident", r)[:, 0:r]).then_inc(vec_turned, 1)

            pe.wait_ge(vec_ok, 2)
            sc = VT[:, 0, 0:32].rearrange("p (s k) -> p k s", s=2)

            def ada(g, s):
                pe.wait_ge(ada_in[s], (g - s) * 2 + 16)
                for k in range(4):
                    kt = 4 * (s % 4) + k
                    o = nc.tensor.matmul(SB[1 + s // 4][0:2, :], sc[:, kt, :], ADA[:, s, k, :],
                                         start=kt == 0, stop=kt == KT - 1)
                o.then_inc(ada_used, 1)

            def ada_loop(lo_, hi_):
                with pe.Fori(lo_, hi_) as i:
                    for s in range(8):
                        if s == 0:
                            pe.wait_ge(ada_ok, i * 2)
                        ada(i * 8 + s, s)

            def ada_turn(b0, b1):
                pe.wait_ge(ada_ok, b1 // 4)
                for b in range(b0, b1):
                    o = nc.tensor.transpose(SB[3][:, 2 * b:2 * b + 2], ADR[:, b * P:(b + 1) * P], con("ident", 2)[:, 0:2])
                o.then_inc(ada_done, 1)

            for s in range(8):
                ada(s, s)
            ada_loop(1, 4)
            ada_turn(0, 28)
            ada_loop(4, 6)
            ada_turn(28, 48)

            pe.wait_ge(xn_ok, 4)

            def turn(kt):
                b = kt % 4
                if kt >= 4:
                    pe.wait_ge(hf_ok, 2 * (kt - 3))
                for t in range(4):
                    o = nc.tensor.transpose(SB[b][:, t * P:(t + 1) * P],
                                            XIN[:, t // 2, t % 2, kt * P:(kt + 1) * P], con("ident"))
                o.then_inc(turned, 1)

            pe.wait_ge(mod_ok, 1)
            for kt in range(4):
                turn(kt)
            for u in range(UPC):
                for kt in (2 * u + 4, 2 * u + 5):
                    if kt < KT:
                        turn(kt)
                pe.wait_ge(h_ok, 2 * u + 2)
                lastu = u == UPC - 1
                done = unit("B0", 0, u, 0, u == 0, lastu)
                if lastu:
                    done[-1][1].then_inc(acc_done[3], 1)
                    pe.wait_ge(acc_done[3], 1)
                    pe.sem_inc(unit_used, 1)
                else:
                    done[-1][1].then_inc(unit_used, 1)

            def turn_ctx_b(k, cb):
                n = 4 * k + cb
                pe.wait_ge(silu_ok, n + 1)
                if n >= 4:
                    pe.wait_ge(t_free, n - 3)
                for t in range(NT):
                    o = nc.tensor.transpose(SB[cb][:, t * P:(t + 1) * P], CV[:, cb, SEQ + t * P:SEQ + (t + 1) * P], con("ident"))
                o.then_inc(t_done, 1)

            def turn_x(n, cb):
                pe.wait_ge(silu_ok, n + 1)
                pe.wait_ge(t_free, n - 3)
                for t in range(4):
                    o = nc.tensor.transpose(SB[cb][:, t * P:(t + 1) * P], CV[:, cb, t * P:(t + 1) * P], con("ident"))
                o.then_inc(t_done, 1)

            def states(k, wait_prev=True):
                pe.wait_ge(xw_ok, k * 2 + 2)
                pe.wait_ge(bg_ok, k + 1)
                for d in range(2):
                    for g in range(2):
                        for t in range(NT):
                            o = nc.tensor.matmul(SB[d][:, g * 256:(g + 1) * 256], BG[:, t, g, :],
                                                 XW[:, d, t, g * 256:(g + 1) * 256], start=t == 0, stop=t == NT - 1)
                    o.then_inc(st_done, 1)

            def cums():
                pe.wait_ge(a_ok, 1)
                a = lambda t, lo, hi: AW[:, 3, t, lo:hi]
                o = None
                for t, d, m0, m1 in ((0, 0, "le", None), (1, 0, "one", "le"), (1, 1, None, "ge"), (0, 1, "ge", "one")):
                    terms = [(m, s) for s, m in ((0, m0), (1, m1)) if m]
                    for x, (m, s) in enumerate(terms):
                        nc.tensor.matmul(SB[2][:, t * 64 + d * 32:t * 64 + d * 32 + 32], con(m), a(s, d * 32, d * 32 + 32),
                                         start=x == 0, stop=x == len(terms) - 1)
                for t, d, m0, m1 in ((0, 0, "gt", "one"), (1, 0, None, "gt"), (0, 1, "lt", None), (1, 1, "one", "lt")):
                    terms = [(m, s) for s, m in ((0, m0), (1, m1)) if m]
                    for x, (m, s) in enumerate(terms):
                        nc.tensor.matmul(SB[2][:, 128 + t * 64 + d * 32:128 + t * 64 + d * 32 + 32], con(m),
                                         a(2 + s, d * 32, d * 32 + 32), start=x == 0, stop=x == len(terms) - 1)
                for d, t, m0, m1 in ((0, 0, "le", None), (0, 1, "one", "le"), (1, 0, "ge", "one"), (1, 1, None, "ge")):
                    terms = [(m, s) for s, m in ((0, m0), (1, m1)) if m]
                    for x, (m, s) in enumerate(terms):
                        o = nc.tensor.matmul(SB[3][0:64, d * 256 + t * P:d * 256 + (t + 1) * P], a(s, 0, 64), con(m),
                                             start=x == 0, stop=x == len(terms) - 1)
                o.then_inc(cums_done, 1)

            def turn_dt():
                pe.wait_ge(dtc_ok, 1)
                for t in range(4):
                    o = nc.tensor.transpose(SB[3][:, t * 64:(t + 1) * 64], DTC[:, t * P:(t + 1) * P], con("ident", 64)[:, 0:64])
                o.then_inc(dt_turned, 1)

            chunk("DT", 1, 0)
            hk = {3 + cb: (lambda cb=cb: turn_ctx_b(0, cb)) for cb in range(3)}
            hk[1] = turn_dt
            hk[6] = lambda: (pe.wait_ge(dtr_ok, 1), turn_ctx_b(0, 3))
            chunk("B1", 2, 0, hooks=hk)
            X0, C0 = chunk0["X"], chunk0["C"]
            hk = {3 + cb: (lambda cb=cb: turn_ctx_b(1, cb)) for cb in range(4)}
            hk[7] = lambda: (pe.wait_ge(t_free, 8), cums())
            chunk("X", X0, 0, hooks=hk)
            chunk("X", X0 + 1, 1, hooks={4 + cb: (lambda cb=cb: turn_x(8 + cb, cb)) for cb in range(4)})
            with pe.Fori(0, 2) as i:
                hk = {4 + cb: (lambda cb=cb: ((pe.wait_ge(st_free, i * 2 + 1 + cb) if cb < 2 else None),
                                              turn_x(i * 4 + 12 + cb, cb))) for cb in range(4)}
                hk[2] = lambda: states(i)
                chunk("X", i + (X0 + 2), 2, i=i, hooks=hk)
            hk = {4 + cb: (lambda cb=cb: ((pe.wait_ge(st_free, 5 + cb) if cb < 2 else None), turn_x(20 + cb, cb)))
                  for cb in range(4)}
            hk[2] = lambda: states(2)
            chunk("C", C0, 0, hooks=hk)
            chunk("C", C0 + 1, 1, hooks={2: lambda: states(3)})

            def turn_ws(x):
                pe.wait_ge(ws_in, 16)
                pe.wait_ge(st_free, 8)
                for g in range(4):
                    o = nc.tensor.transpose(SB[x][:, g * P:(g + 1) * P], WS[:, 4 * x + g, :], con("ident"))
                o.then_inc(ws_turned, 1)

            def mix(x):
                pe.wait_ge(vn_ok, 4)
                pe.wait_ge(ws_ok, 4)
                if x >= 4:
                    pe.wait_ge(sg_ok, x - 3)
                for y in range(2):
                    g = 2 * x + y
                    o = nc.tensor.matmul(SB[x % 4][:, y * 256:(y + 1) * 256].rearrange("p (t e) -> p t e", t=NT),
                                         WST[:, g, :], V[:, :, g * P:(g + 1) * P], start=True, stop=True)
                o.then_inc(sg_done, 1)

            def ssd_cb(g):
                pe.wait_ge(gb_ok, g + 1)
                if not isinstance(g, int) or g:
                    pe.wait_ge(y_ok, g)
                else:
                    pe.wait_ge(sg_ok, 8)
                for t in range(NT):
                    o = nc.tensor.matmul(SB[2][:, t * SEQ:(t + 1) * SEQ], GB[:, 0, t * P:(t + 1) * P], GB[:, 1, :],
                                         start=True, stop=True)
                o.then_inc(cb_done, 1)
                ssd_off(g, 0)

            def ssd_off(g, d):
                if d:
                    pe.wait_ge(yo_used, g * 2 + 1)
                for t in range(NT):
                    o = nc.tensor.matmul(SB[3][:, t * 256:(t + 1) * 256], GB[:, 1, t * P:(t + 1) * P],
                                         ST[:, d, bass.ds(g * 256, 256)], start=True, stop=True)
                o.then_inc(yo_done, 1)

            def ssd_rows(g, r):
                if not (isinstance(g, int) and g == 0 and r == 0):
                    pe.wait_ge(e_ok, g * 4 + r)
                for d in range(2):
                    one = SEL[:, d, r:r + 1].to_broadcast([64, P])
                    if d == 0:
                        spans = ((0, 0, 256, 0), (256, 128, 128, 256))
                    else:
                        spans = ((0, 0, 256, 128), (256, 0, 128, 256))
                    for o0, q0, n, m0 in spans:
                        nc.tensor.matmul(SB[d][:, o0:o0 + n], one, ART[:, 0, q0:q0 + n], start=True, stop=False)
                        nc.tensor.matmul(SB[d][:, m0:m0 + P], IDR[:], NEGR[:, d, :], start=False, stop=False,
                                         skip_group_check=True)
                        o = nc.tensor.matmul(SB[d][:, o0:o0 + n], one, ART[:, 1, q0:q0 + n], start=False, stop=True)
                o.then_inc(r_done, 1)

            def ssd_y(g, r):
                pe.wait_ge(m_ok, g * 4 + r + 1)
                for t in range(NT):
                    for k in range(NT):
                        o = nc.tensor.matmul(SB[2][:, t * 256 + r * HD:t * 256 + (r + 1) * HD],
                                             MM[:, r % 2, k, t * P:(t + 1) * P],
                                             XH[:, k, bass.ds(g * 256 + r * HD, HD)], start=k == 0, stop=k == NT - 1)
                o.then_inc(y_done, 1)

            def ssd_hooks(g):
                hk = {0: lambda: ssd_cb(g), 1: lambda: (ssd_off(g, 1), ssd_rows(g, 0)), 2: lambda: ssd_rows(g, 1),
                      3: lambda: (ssd_y(g, 0), ssd_rows(g, 2)), 4: lambda: (ssd_y(g, 1), ssd_rows(g, 3)),
                      5: lambda: ssd_y(g, 2), 6: lambda: ssd_y(g, 3)}
                return hk

            cV, cU, cM, cS, cO = (chunk0[n] for n in ("V", "U", "M", "S", "O1"))
            chunk("V", cV, 0)
            chunk("V", cV + 1, 1, hooks={u: (lambda u=u: turn_ws(u)) for u in range(4)})
            chunk("V", cV + 2, 2)
            chunk("V", cV + 3, 3)
            chunk("U", cU, 0, hooks={7: lambda: [mix(x) for x in range(4)]})
            chunk("U", cU + 1, 1, hooks={1: lambda: [mix(x) for x in range(4, 8)]})
            chunk("U", cU + 2, 2, hooks=ssd_hooks(0))
            chunk("U", cU + 3, 3, hooks=ssd_hooks(1))
            with pe.Fori(0, 2) as i:
                for j in range(2):
                    chunk("M", i * 2 + (cM + j), j, i=i, hooks=ssd_hooks(i * 2 + (2 + j)))
            chunk("S", cS, 0, hooks=ssd_hooks(6))
            chunk("S", cS + 1, 1, hooks=ssd_hooks(7))

            def gate_rows(b):
                pe.wait_ge(y_ok, 8)
                for k in range(4):
                    o = nc.tensor.matmul(SB[b][:, k * P:(k + 1) * P], MOD[:, 4, 4 * b + k:4 * b + k + 1].to_broadcast([P, P]),
                                         con("ident"), start=True, stop=True)
                o.then_inc(gg_done, 1)

            def turn_half(src, ok, n_ok, x, k0, prior):
                b = x % 4
                pe.wait_ge(ok, n_ok)
                if x >= 4:
                    pe.wait_ge(h_lo, 16 * k0 + 2 * (x - 3))
                else:
                    pe.wait_ge(prior[0], prior[1])
                for k in range(2):
                    for t in range(NT):
                        kt = 2 * x + k
                        o = nc.tensor.transpose(SB[b][:, k * SEQ + t * P:k * SEQ + (t + 1) * P], src[:, t, kt * P:(kt + 1) * P], con("ident"))
                o.then_inc(h_turned, 1)

            hk = {b: (lambda b=b: gate_rows(b)) for b in range(4)}
            hk[7] = lambda: turn_half(T, tn_ok, 2, 0, 0, (gg_ok, 4))
            chunk("S", cS + 2, 2, hooks=hk)
            hk = {u: (lambda u=u: turn_half(T, tn_ok, 2, u + 1, 0, (gg_ok, 4))) for u in range(7)}
            chunk("S", cS + 3, 3, hooks=hk)
            pe.wait_ge(h_lo, 16)
            chunk("O1", cO, 0, kt0=KT, last=False, pair=0)
            for x in range(8):
                turn_half(Y, yn_ok, 2, x, 1, (h_lo, 16))
            pe.wait_ge(h_lo, 32)
            chunk("O1", cO + 1, 1, first=False, pair=0)
            chunk("O1", cO + 2, 2, kt0=KT, last=False, pair=1)
            chunk("O1", cO + 3, 3, first=False, pair=1)
            chunk("O1", cO + 4, 4, kt0=KT, last=False, pair=0)
            chunk("O1", cO + 5, 5, first=False, pair=0)
            chunk("O1", cO + 6, 6, kt0=KT, last=False, pair=1)
            chunk("O1", cO + 7, 7, first=False, pair=1)



            def head_chunk(L, ph, c, mode=None, hooks={}, prior=None):
                tn = lambda x: turn_half(XN, nxn_ok, 2 * L + 2, x, L + 2, prior)
                for x in range(4):
                    tn(x)

                def ahead(u):
                    if u + 4 < UPC:
                        tn(u + 4)
                    pe.wait_ge(h_lo, 16 * (L + 2) + 2 * u + 2)
                chunk(ph, c, 0, ahead={u: (lambda u=u: ahead(u)) for u in range(UPC)}, hooks=hooks)

            def att_level(hb, l):
                n = hb * 9 + l
                if l == 0:
                    pe.wait_ge(ki_ok, hb + 1)
                    pe.wait_ge(bq_ok, hb + 1)
                    pe.wait_ge(h_lo, 48)
                else:
                    pe.wait_ge(wl_ok, 8 * hb + l)
                if n >= 2:
                    hb_, l_ = divmod(n - 2, 9)
                    pe.wait_ge(*((aw_ok, hb_ + 1) if l_ == 8 else (at_ok, 8 * hb_ + l_ + 1)))
                for h in range(4):
                    if l == 8:
                        o = nc.tensor.matmul(SB[2 * (n % 2)][:, h * P:(h + 1) * P], WL[:, l % 2, h, 0:P],
                                             WL[:, l % 2, h, P:], start=True, stop=True)
                        continue
                    b, o0 = SB[2 * (n % 2) + h // 2], (h % 2) * 256
                    for k in range(NT):
                        sl = slice(k * P, (k + 1) * P)
                        l_, r_ = (KI[:, hb, h, sl], BQ_[:, hb, h, sl]) if l == 0 else (WL[:, l % 2, h, sl],) * 2
                        o = nc.tensor.matmul(b[:, o0 + k * P:o0 + (k + 1) * P], l_, r_, start=True, stop=True)
                o.then_inc(at_done, 1)

            def turn_q(n):
                pe.wait_ge(rope_ok, 1)
                pe.wait_ge(at_ok, 16)
                pe.wait_ge(aw_ok, 2)
                if n >= 4:
                    pe.wait_ge(qt_ok, n - 3)
                at_ = 16 if n == 0 else 2 * (n - 1)
                for y in range(2):
                    for t in range(NT):
                        o = nc.tensor.transpose(SB[n % 4][0:64, y * SEQ + t * P:y * SEQ + (t + 1) * P],
                                                AQ[:, t, (at_ + y) * 64:(at_ + y + 1) * 64], con("ident"))
                o.then_inc(aq_turned, 1)

            def side_bank(n):
                pe.wait_ge(qt_ok, 9)
                if n >= 2:
                    pe.wait_ge(side_free, n - 1)
                return SB[n % 2]

            def scores(h):
                b = side_bank(SIDE_USER["scores", h])
                for o0, qb, kb_ in ((0, 0, 0), (128, 1, 0), (256, 1, 1)):
                    o = nc.tensor.matmul(b[:, o0:o0 + P], QT[:, h, qb * P:(qb + 1) * P], KTT[:, h // 8, kb_ * P:(kb_ + 1) * P],
                                         start=True, stop=True)
                o.then_inc(sc_done, 1)

            def turn_p(h):
                pe.wait_ge(pe_ok, h + 1)
                if h >= 2:
                    pe.wait_ge(ya_ok, h - 1)
                for k in range(3):
                    o = nc.tensor.transpose(SB[2 + h % 2][:, k * P:(k + 1) * P], PA[:, h % 2, k * P:(k + 1) * P], con("ident"))
                o.then_inc(pt_done, 1)

            def attend(h):
                pe.wait_ge(pt_ok, h + 1)
                b, v = SB[2 + h % 2], (h // 8) * 64
                nc.tensor.matmul(b[:, 384:448], PT[:, h % 2, 0, :], AV[:, 0, v:v + 64], start=True, stop=True)
                nc.tensor.matmul(b[:, 448:512], PT[:, h % 2, 1, :], AV[:, 0, v:v + 64], start=True, stop=False)
                nc.tensor.matmul(b[:, 448:512], PT[:, h % 2, 2, :], AV[:, 1, v:v + 64], start=False, stop=True).then_inc(pv_done, 1)

            def hgrn_out(g2):
                b = side_bank(SIDE_USER["hgrn", g2])
                pe.wait_ge(bi_ok, 4 if g2 >= 2 else 2)
                for y in range(2):
                    g = 2 * g2 + y
                    hb, h = g // 4, g % 4
                    v = [BI_[:, t, g * P:(g + 1) * P] for t in range(NT)]
                    o0 = y * 256
                    nc.tensor.matmul(b[:, o0:o0 + P], ATT[:, hb, h, 0, :], v[0], start=True, stop=True)
                    nc.tensor.matmul(b[:, o0 + P:o0 + 256], ATT[:, hb, h, 1, :], v[1], start=True, stop=False)
                    o = nc.tensor.matmul(b[:, o0 + P:o0 + 256], AT8[:, hb, h, :], v[0], start=False, stop=True)
                o.then_inc(ob_done, 1)

            def turn_y(x):
                b = side_bank(SIDE_USER["turn", x])
                if x < 4:
                    pe.wait_ge(yb_ok, 1)
                    src, k0 = OB, 2 * x
                else:
                    pe.wait_ge(gate_free, 24 if x < 6 else 26)
                    src, k0 = YA, 2 * (x - 4)
                for k in range(2):
                    for t in range(NT):
                        o = nc.tensor.transpose(b[:, k * SEQ + t * P:k * SEQ + (t + 1) * P],
                                                src[:, t, (k0 + k) * P:(k0 + k + 1) * P], con("ident"))
                o.then_inc(y2_turned, 1)

            def side2(b):
                for hb, b0 in ((0, LEV0), (1, LEV1)):
                    if b0 - 1 <= b <= b0 + 15 and (b - b0) % 2:
                        att_level(hb, (b - b0 + 1) // 2)
                if 62 <= b <= 64:
                    for n in range(3):
                        turn_q(3 * (b - 62) + n)
                for h in range(A_H):
                    if b == HEAD_BEAT + 2 * h + 6:
                        attend(h)
                    if b == HEAD_BEAT + 2 * h + 3:
                        turn_p(h)
                    if b == HEAD_BEAT + 2 * h:
                        scores(h)
                for g2 in range(4):
                    if b == HGRN_BEAT + 2 * g2:
                        hgrn_out(g2)
                for x in range(8):
                    if b == TURN_BEAT[x]:
                        turn_y(x)

            C2 = chunk0["BF0"]
            beats2 = lambda c: {u: (lambda u=u: side2(8 * c + u)) for u in range(UPC)}
            head_chunk(0, "BF0", C2, hooks={}, prior=(h_lo, 32))
            cc = 1
            for ph in ("BQ0", "BF1", "BQ1", "AK", "AQ", "BI", "BG", "AG"):
                for j in range(count_of[ph]):
                    chunk(ph, C2 + cc, j, hooks=beats2(cc))
                    cc += 1
            chunk("O2", C2 + cc, 0, kt0=1, turn=8, hooks=beats2(cc),
                  ahead={u: (lambda u=u: pe.wait_ge(y2_lo, 2 * u + 2)) for u in range(UPC)})
            for j in range(1, 4):
                chunk("O2", C2 + cc + j, j, kt0=1, turn=8)


            def stick_scores(h):
                pe.wait_ge(qk_ok, 4 * (h // 4) + 4)
                pe.wait_ge(h_lo, 64)
                pe.wait_ge(n3_ok, 1)
                if h >= 2:
                    pe.wait_ge(w3_ok, h - 1)
                b, q, k = SB[h % 2], QF[:, h // 4 % 2, h % 4], KF[:, h // 4 % 2, h % 4]
                nc.tensor.matmul(b[:, 0:256], k[:, 0:P], q, start=True, stop=True)
                nc.tensor.matmul(b[:, 256:384], k[:, P:], q[:, P:], start=False, stop=True, skip_group_check=True)
                for o0 in (0, 256):
                    o = nc.tensor.matmul(b[:, o0:o0 + P], IDR[:], NM3[:], start=False, stop=True, skip_group_check=True)
                o.then_inc(z_done, 1)

            def stick_sums(h):
                pe.wait_ge(spm_ok, h + 1)
                b, s = SB[h % 2], SPM[:, h % 2].rearrange("p k q -> p (k q)")
                nc.tensor.matmul(b[:, 0:384], NEG3[:, 0, :], s, start=False, stop=True, skip_group_check=True)
                nc.tensor.matmul(b[:, 128:256], NEG3[:, 1, :], s[:, 256:384], start=False, stop=True,
                                 skip_group_check=True).then_inc(sum_done, 1)

            def side_bank3(n):
                if n >= 2:
                    pe.wait_ge(side_free, 28 + n - 1)
                return SB[2 + n % 2]

            def stick_out(h):
                pe.wait_ge(w3_ok, h + 1)
                pe.wait_ge(cv_ok, 2 * (h // 4) + 2)
                b, w = side_bank3(SIDE3_USER["out", h]), W3[:, h % 2]
                v = [VF[:, h // 4 % 2, t, (h % 4) * P:(h % 4 + 1) * P] for t in range(NT)]
                nc.tensor.matmul(b[:, 0:P], w[:, 0], v[0], start=True, stop=True)
                nc.tensor.matmul(b[:, P:256], w[:, 1], v[0], start=True, stop=False)
                nc.tensor.matmul(b[:, P:256], w[:, 2], v[1], start=False, stop=True).then_inc(oc_done, 1)

            def turn_y3(x):
                b = side_bank3(SIDE3_USER["turn", x])
                pe.wait_ge(gate_free, 2 * (x // 2) + 28)
                for k in range(2):
                    for t in range(NT):
                        o = nc.tensor.transpose(b[:, k * SEQ + t * P:k * SEQ + (t + 1) * P],
                                                OC[:, t, (2 * x + k) * P:(2 * x + k + 1) * P], con("ident"))
                o.then_inc(y2_turned, 1)

            def side3(b):
                for h in range(C_H):
                    if b == STICK_BEAT + 6 * h + 6:
                        stick_out(h)
                    if b == STICK_BEAT + 6 * h + 3:
                        stick_sums(h)
                    if b == STICK_BEAT + 6 * h:
                        stick_scores(h)
                for x in range(8):
                    if b == TURN3_BEAT[x]:
                        turn_y3(x)

            C3 = chunk0["CQ0"]
            beats3 = lambda cc: {u: (lambda u=u: side3(8 * cc + u)) for u in range(UPC)}
            head_chunk(1, "CQ0", C3, prior=(y2_lo, 16))
            chunk("CK0", C3 + 1, 0)
            chunk("CV0", C3 + 2, 0)
            for j in range(9):
                chunk("CR", C3 + 3 + j, j, mode="tok" if j % 3 == 2 else "feat", hooks=beats3(3 + j))
            for j in range(4):
                chunk("CG", C3 + 12 + j, j, hooks=beats3(12 + j))
            chunk("O3", C3 + 16, 0, kt0=KT, hooks=beats3(16),
                  ahead={u: (lambda u=u: pe.wait_ge(y2_lo, 16 + u + 1)) for u in range(UPC)})
            for j in range(1, 4):
                chunk("O3", C3 + 16 + j, j, kt0=KT)

        @block.scalar
        def _(act):
            seq = Seq(act, act_seq)

            def hi(c, u, n):
                act.wait_ge(raw_in[u % 4], (c * 2 + (u // 4 + 1)) * 16)
                if not (isinstance(c, int) and c * UPC + u < 4):
                    act.wait_ge(unit_used, c * UPC + (u - 3))
                act.copy(WHI[:, u % 4, :, 0:n], RAW[:, u % 4, :, 0:n]).then_inc(hi_ready, 1)

            act.wait_ge(vec_turned, 4)
            act.activation(VT[:, 0, 0:32], SB[0][:, 0:32], ACT.Silu).then_inc(vec_ok, 1)
            rest = VEC_ROWS
            act.copy(VT[:, 0, 32:P], SB[0][:, 32:P])
            act.copy(VT[:, 1, 0:rest[1]], SB[0][:, P:P + rest[1]])
            act.copy(VT[:, 2], SB[0][:, 2 * P:3 * P])
            act.copy(VT[:, 3, 0:rest[3]], SB[0][:, 3 * P:3 * P + rest[3]]).then_inc(vec_ok, 1)
            act.copy(IDR[:], con("ident")).then_inc(r_const, 1)
            act.copy(NEGR[:], CON[:, CAT["neg_f"]:CAT["neg_f"] + 256].rearrange("p (a b) -> p a b", a=2)).then_inc(r_const, 1)
            act.wait_ge(x_in, 32)
            for t in range(4):
                if t:
                    act.wait_ge(ssq_ok, t)
                act.activation(JUNK[:], XIN[:, t // 2, t % 2, :], ACT.Square, accum_out=STAT[:, t:t + 1]).then_inc(ssq_ok, 1)
            act.wait_ge(std_ok, 1)
            act.activation(STAT[:, 8:12], STAT[:, 4:8], ACT.Sqrt).then_inc(std_ok, 1)
            for u in range(3):
                hi(0, u, NCOL)
            act.wait_ge(mod_ok, 1)
            for kt in range(KT):
                act.wait_ge(turned, kt + 1)
                if kt >= 2:
                    act.wait_ge(h_ok, kt - 1)
                b = SB[kt % 4]
                act.activation(HF[:, kt % 2, 0:SEQ], b[:, 0:SEQ], ACT.Identity, scale=MOD[:, 0, kt:kt + 1],
                               bias=MOD[:, 2, kt:kt + 1]).then_inc(hf_ok, 1)
                act.activation(HF[:, kt % 2, SEQ:], b[:, SEQ:], ACT.Identity, scale=MOD[:, 1, kt:kt + 1],
                               bias=MOD[:, 3, kt:kt + 1]).then_inc(hf_ok, 1)
                if kt in (4, 7, 10, 13, 15):
                    hi(0, 3 + (4, 7, 10, 13, 15).index(kt), NCOL)
            for u in range(3):
                hi(1, u, NCOL)

            def evict_wide(n, c, i=0, ph="B0", j=0):
                for b in range(4):
                    act.wait_ge(acc_done[b], before[ph, j][b] + 1 + i)
                    if not (isinstance(n, int) and n == 0):
                        act.wait_ge(conv_ok, n + b - 3)
                    act.copy(ZB[:, b, :], ACC[b][:]).then_inc(z_ok, 1)
                    act.wait_ge(z_ok, n + b + 1)
                    act.sem_inc(acc_free[b], 1)

            def evict_feat(n, ph, j):
                for b4 in range(4):
                    b = 2 * (j % 2) + b4 // 2
                    act.wait_ge(acc_done[b], before[ph, j][b] + 1)
                    act.wait_ge(conv_ok, n + b4 - 3)
                    act.copy(ZB[:, b4, 0:SEQ], ACC[b][:, (b4 % 2) * SEQ:(b4 % 2 + 1) * SEQ]).then_inc(z_ok, 1)
                    if b4 % 2:
                        act.wait_ge(z_ok, n + b4 + 1)
                        act.sem_inc(acc_free[b], 1)

            def silu_b(k, cb):
                n = 4 * k + cb
                act.wait_ge(conv_ok, n + 1)
                act.activation(BT[:, n, :], CV[:, cb, 0:SEQ], ACT.Silu)
                act.activation(CV[:, cb, SEQ:], CV[:, cb, SEQ:], ACT.Silu).then_inc(silu_ok, 1)

            def silu_x(n, cb):
                act.wait_ge(conv_ok, n + 1)
                act.activation(CV[:, cb, :], CV[:, cb, :], ACT.Silu).then_inc(silu_ok, 1)

            def silu_c(k, cb):
                n = 24 + 4 * k + cb
                act.wait_ge(conv_ok, n + 1)
                if k == 0 and cb == 0:
                    act.wait_ge(st_done, 8)
                act.activation(CT[:, 4 * k + cb, :], CV[:, cb, 0:SEQ], ACT.Silu).then_inc(silu_ok, 1)

            def dt_exp():
                act.wait_ge(dtr_ok, 2)
                act.activation(AW[:, 1], AW[:, 1], ACT.Exp, scale=-1.0).then_inc(dte_ok, 1)
                act.activation(AW[:, 2, 0], BCS[:, 64:128], ACT.Exp)
                act.wait_ge(dte_ok, 1)
                act.activation(AW[:, 1], AW[:, 1], ACT.Ln, bias=1.0).then_inc(dtl_ok, 1)

            def cum_out():
                act.wait_ge(cums_done, 1)
                s = SB[2][:, 0:128].rearrange("p (t h) -> p t h", t=NT)
                act.copy(ACS[:, 0], s).then_inc(cums_ok, 1)
                act.activation(ACS[:, 1], s, ACT.Copy, scale=-1.0).then_inc(cums_ok, 1)
                act.activation(ACS[:, 2], s, ACT.Exp).then_inc(cums_ok, 1)
                act.activation(WCX[:], SB[2][:, 128:256].rearrange("p (t h) -> p t h", t=NT), ACT.Exp).then_inc(cums_ok, 1)
                act.copy(ART[0:32, 0, :], SB[3][0:32, 0:256])
                act.copy(ART[32:64, 0, :], SB[3][32:64, 256:512]).then_inc(cums_ok, 1)

            def states_out(k):
                act.wait_ge(st_done, k * 2 + 1)
                for d in range(2):
                    act.wait_ge(st_done, k * 2 + d + 1)
                    act.copy(ST[:, d, bass.ds(k * 512, 512)], SB[d][:]).then_inc(st_free, 1)

            H = lambda f, *a: (lambda: f(*a))
            def dt_evict():
                act.wait_ge(acc_done[0], before["DT", 0][0] + 1)
                act.copy(DTC[:], ACC[0][0:64, :]).then_inc(dtc_ok, 1)
                act.wait_ge(dtc_ok, 1)
                act.sem_inc(acc_free[0], 1)

            evict_wide(0, 0)
            split_steps(act, hi, "DT", 1, 0, {}, dt_evict)
            split_steps(act, hi, "B1", 2, 0, {4 + cb: H(silu_b, 0, cb) for cb in range(4)},
                        H(evict_wide, 4, 2, 0, "B1", 0))
            X0, C0 = chunk0["X"], chunk0["C"]
            mid = {4 + cb: H(silu_b, 1, cb) for cb in range(4)}
            mid[3] = dt_exp
            mid[9] = cum_out
            split_steps(act, hi, "X", X0, 0, mid, H(evict_wide, 8, X0, 0, "X", 0))
            split_steps(act, hi, "X", X0 + 1, 1, {4 + cb: H(silu_x, 8 + cb, cb) for cb in range(4)},
                        H(evict_wide, 12, X0 + 1, 0, "X", 1))
            with act.Fori(0, 2) as i:
                mid = {4 + cb: H(silu_x, i * 4 + 12 + cb, cb) for cb in range(4)}
                mid[3] = H(states_out, i)
                split_steps(act, hi, "X", i + (X0 + 2), 0, mid, H(evict_wide, i * 4 + 16, 0, i, "X", 2))
            mid = {4 + cb: H(silu_x, 20 + cb, cb) for cb in range(4)}
            mid[3] = H(states_out, 2)
            split_steps(act, hi, "C", C0, 0, mid, H(evict_feat, 24, "C", 0))
            mid = {4 + cb: H(silu_c, 0, cb) for cb in range(4)}
            mid[3] = H(states_out, 3)
            split_steps(act, hi, "C", C0 + 1, 1, mid, H(evict_feat, 28, "C", 1))

            def acc_wait(ph, j, b, i=0):
                act.wait_ge(acc_done[b], before[ph, j][b] + 1 + i)

            def v_out(j):
                for t in range(NT):
                    b = 2 * (j % 2) + t
                    acc_wait("V", j, b)
                    act.copy(V[:, t, j * NCOL:(j + 1) * NCOL], ACC[b][:])
                    act.activation(ACC[b][:], ACC[b][:], ACT.Square,
                                   accum_out=STAT[:, 16 + 4 * t + j:17 + 4 * t + j]).then_inc(v_ok, 1)
                    act.wait_ge(v_ok, 2 * j + t + 1)
                    act.sem_inc(acc_free[b], 1)

            def v_std():
                act.wait_ge(vstd_ok, 1)
                act.activation(STAT[:, 26:28], STAT[:, 24:26], ACT.Sqrt).then_inc(vstd_ok, 1)

            def mixed(x):
                act.wait_ge(sg_done, x + 1)
                for y in range(2):
                    g = 2 * x + y
                    o = act.activation(T[:, :, g * P:(g + 1) * P], SB[x % 4][:, y * 256:(y + 1) * 256].rearrange("p (t e) -> p t e", t=NT),
                                       ACT.Identity, bias=vec("b_s", g))
                o.then_inc(sg_ok, 1)

            def cb_out(g):
                act.wait_ge(cb_done, g + 1)
                act.copy(CBS[:], SB[2][:].rearrange("p (k q) -> p k q", k=NT)).then_inc(cbs_ok, 1)

            def exps(g, r):
                act.wait_ge(r_done, g * 4 + r + 1)
                if not (isinstance(g, int) and g * 4 + r < 2):
                    act.wait_ge(m_ok, g * 4 + r - 1)
                e = EX[:, r % 2]
                for d, k, o0, n, to in ((0, 0, 0, 256, 0), (0, 1, 256, P, 256), (1, 0, 256, P, 384), (1, 1, 0, 256, 512)):
                    o = act.activation(e[:, to:to + n], SB[d][:, o0:o0 + n], ACT.Exp,
                                       bias=ACS[:, 1, k, bass.ds(g * 4 + (32 * d + r), 1)])
                o.then_inc(e_ok, 1)

            def ssd_mid(g):
                return {3: H(cb_out, g), 4: H(exps, g, 0), 5: H(exps, g, 1), 6: H(exps, g, 2), 7: H(exps, g, 3)}

            def gate_out(ph, j, i=0, n=0):
                for t in range(NT):
                    b = 2 * (j % 2) + t
                    acc_wait(ph, j, b, i)
                    k = n + t
                    act.wait_ge(gate_free, k + 1)
                    act.activation(SG[:, t], ACC[b][:], ACT.Silu).then_inc(gate_ok, 1)
                    act.wait_ge(gate_ok, k + 1)
                    act.sem_inc(acc_free[b], 1)

            cV, cU, cM, cS, cO = (chunk0[n] for n in ("V", "U", "M", "S", "O1"))
            nothing = lambda: None
            split_steps(act, hi, "V", cV, 0, {4 + cb: H(silu_c, 1, cb) for cb in range(4)}, H(v_out, 0))
            for j in range(1, 4):
                split_steps(act, hi, "V", cV + j, j, {}, H(v_out, j))
            split_steps(act, hi, "U", cU, 0, {3: v_std}, lambda: [mixed(x) for x in range(4)])
            split_steps(act, hi, "U", cU + 1, 1, {3: lambda: [mixed(x) for x in range(4, 8)]}, nothing)
            split_steps(act, hi, "U", cU + 2, 2, ssd_mid(0), nothing)
            split_steps(act, hi, "U", cU + 3, 3, ssd_mid(1), nothing)
            with act.Fori(0, 2) as i:
                for j in range(2):
                    split_steps(act, hi, "M", i * 2 + (cM + j), j, ssd_mid(i * 2 + (2 + j)),
                                H(gate_out, "M", j, i, i * 4 + 2 * j))
            split_steps(act, hi, "S", cS, 0, ssd_mid(6), H(gate_out, "S", 0, 0, 8))
            split_steps(act, hi, "S", cS + 1, 1, ssd_mid(7), H(gate_out, "S", 1, 0, 10))

            def squares(src, ok, n_ok, col, done_, n_prev=0):
                act.wait_ge(ok, n_ok)
                for t in range(NT):
                    for q in range(4):
                        if n_prev + 4 * t + q:
                            act.wait_ge(done_, n_prev + 4 * t + q)
                        act.activation(DUMP[:], src[:, t, q * NCOL:(q + 1) * NCOL], ACT.Square,
                                       accum_out=STAT[:, col + 4 * t + q:col + 4 * t + q + 1]).then_inc(done_, 1)

            def root(s, c):
                act.wait_ge(s, 1)
                act.activation(STAT[:, c + 2:c + 4], STAT[:, c:c + 2], ACT.Sqrt).then_inc(s, 1)

            def gate_row_out(b):
                act.wait_ge(gg_done, b + 1)
                act.copy(GG[:, b * NCOL:(b + 1) * NCOL], SB[b][:]).then_inc(gg_ok, 1)

            def half_hi(dst, gname, x, k0):
                act.wait_ge(h_turned, 8 * k0 + x + 1)
                for k in range(2):
                    kt = 2 * x + k
                    act.activation(dst[:, kt, :], SB[x % 4][:, k * SEQ:(k + 1) * SEQ], ACT.Copy,
                                   scale=vec(gname, kt)).then_inc(h_hi, 1)

            def y_squares(j):
                act.wait_ge(yg_ok, 2 * j + 2)
                for t in range(NT):
                    if j or t:
                        act.wait_ge(ysq_ok, 2 * j + t)
                    act.activation(DUMP[:], Y[:, t, j * NCOL:(j + 1) * NCOL], ACT.Square,
                                   accum_out=STAT[:, 44 + 4 * t + j:45 + 4 * t + j]).then_inc(ysq_ok, 1)

            split_steps(act, hi, "S", cS + 2, 2, {3: H(squares, T, t_ok, 8, 32, tsq_ok),
                                                  5: lambda: (root(tstd_ok, 40), y_squares(0)), 8: lambda: [gate_row_out(b) for b in range(4)]},
                        H(gate_out, "S", 2, 0, 12))
            mid = {u: H(half_hi, GHI, "g_mlp", u - 3, 0) for u in range(3, 8)}
            mid[8] = H(half_hi, GHI, "g_mlp", 5, 0)
            mid[9] = H(half_hi, GHI, "g_mlp", 6, 0)
            mid[10] = lambda: (half_hi(GHI, "g_mlp", 7, 0), y_squares(1), y_squares(2))
            split_steps(act, hi, "S", cS + 3, 3, mid, H(gate_out, "S", 3, 0, 14))
            y_squares(3)
            root(ystd_ok, 52)
            for u in range(3, 8):
                hi(cO, u, NCOL)
            for x in range(8):
                half_hi(HHI[:, 0], "g_ssd", x, 1)
            for u in range(3):
                hi(cO + 1, u, NCOL)

            def o_out(r):
                for t in range(NT):
                    b = 2 * (r % 2) + t
                    j = 2 * r + 1
                    acc_wait("O1", j, b)
                    if r or t:
                        act.wait_ge(osq_ok, 2 * r + t)
                    act.activation(DUMP[:], ACC[b][:], ACT.Square,
                                   accum_out=STAT[:, 16 + 4 * t + r:17 + 4 * t + r]).then_inc(osq_ok, 1)

            for r in range(4):
                if r:
                    split_steps(act, hi, "O1", cO + 2 * r, 2 * r, {}, nothing)
                split_steps(act, hi, "O1", cO + 2 * r + 1, 2 * r + 1, {}, H(o_out, r))
            root(ostd_ok, 56)

            def norm_in(L, n):
                for t in range(NT):
                    act.wait_ge(x_ok, n + (2 if L else t + 1))
                    act.activation(XN[:, t], X1[:, t], ACT.Square, accum_out=ST3[:, t:t + 1]).then_inc(nsq_ok, 1)
                act.wait_ge(nrt_ok, 2 * L + 1)
                act.activation(ST3[:, 4:6], ST3[:, 2:4], ACT.Sqrt).then_inc(nrt_ok, 1)

            def head_steps(L, c, n, half):
                hi(c, 3, n)
                for x in range(4):
                    half(x)
                for u in range(4, 8):
                    half(u)
                    hi(c, u, n)

            C2 = chunk0["BF0"]
            norm_in(0, 0)
            head_steps("even", C2, NCOL, lambda x: half_hi(HHI[:, 0], "ln_even_2", x, 2))

            def lower_bound():
                act.wait_ge(lb_sem, 1)
                act.activation(LBC[:, 5], LBC[:, 5], ACT.Exp).then_inc(lb_sem, 1)
                act.wait_ge(lb_sem, 3)
                act.activation(LBC[:, 3], LBC[:, 1], ACT.Ln)
                act.activation(LBC[:, 4], LBC[:, 5], ACT.Ln, scale=2.0 ** 64).then_inc(lb_sem, 1)

            def free_pair(ph, j, s, n):
                act.wait_ge(s, n)
                for b in banks_of(ph, mode_of[ph], j):
                    act.sem_inc(acc_free[b], 1)

            def bf_out(hb):
                ph = f"BF{hb}"
                if hb:
                    act.wait_ge(logf_ok, 1)
                for y in range(2):
                    b = 2 * pair_of(ph, 0) + y
                    acc_wait(ph, 0, b)
                    half = lambda T_: T_[:, hb, 2 * y:2 * y + 2, :].rearrange("p h t -> p (h t)")
                    act.copy(P1[:, 2 * y:2 * y + 2, :].rearrange("p h t -> p (h t)"), ACC[b][:])
                    act.activation(half(KI), ACC[b][:], ACT.Sigmoid, scale=-1.0)
                    seq(act.activation(half(VV), ACC[b][:], ACT.Abs))
                    act.sem_inc(acc_free[b], 1)
                seq(act.activation(VV[:, hb], VV[:, hb], ACT.Exp, scale=-1.0))
                act.activation(VV[:, hb], VV[:, hb], ACT.Ln, bias=1.0).then_inc(p1_ok, 1)

            def log_add(hb):
                act.wait_ge(la_ok, hb + 1)
                seq(act.activation(P1[:], P1[:], ACT.Exp, scale=-1.0))
                act.activation(P1[:], P1[:], ACT.Ln, bias=1.0).then_inc(lx_ok, 1)

            def bq_out(hb):
                ph = f"BQ{hb}"
                for y in range(2):
                    b = 2 * pair_of(ph, 0) + y
                    acc_wait(ph, 0, b)
                    o = act.activation(BQ_[:, hb, 2 * y:2 * y + 2, :].rearrange("p h t -> p (h t)"), ACC[b][:], ACT.Silu)
                    if y:
                        o.then_inc(bq_ok, 1)
                        act.wait_ge(bq_ok, hb + 1)
                    else:
                        seq(o)
                    act.sem_inc(acc_free[b], 1)

            def level_exp(hb, l):
                n = 8 * hb + l
                if l == 1:
                    act.wait_ge(logf_ok, hb + 1)
                else:
                    act.wait_ge(uv_ok, 7 * hb + l - 1)
                if n >= 3:
                    m = (n - 2 - 1)
                    act.wait_ge(at_done, 9 * (m // 8) + m % 8 + 2)
                for src, up in ((U_, 1), (VV, 0)):
                    act.activation(level(WL[:, l % 2], l, up), level(src[:, hb], l, up), ACT.Exp).then_inc(we_ok, 1)

            def att_wide(hb):
                n = hb * 9 + 8
                act.wait_ge(at_done, n + 1)
                act.copy(AT8[:, hb], SB[2 * (n % 2)][:].rearrange("p (h q) -> p h q", h=4)).then_inc(aw_ok, 1)

            def ak_out():
                for t in range(NT):
                    b = 2 * pair_of("AK", 0) + t
                    acc_wait("AK", 0, b)
                    act.copy(AQ[:, t, 1024:1152], ACC[b][:, 0:128])
                    act.copy(AV[:, t, :], ACC[b][:, 128:256]).then_inc(aq_ok, 1)
                    act.wait_ge(aq_ok, t + 1)
                    act.sem_inc(acc_free[b], 1)

            def tok_out(ph, j, dst, s, n):
                for t in range(NT):
                    b = 2 * pair_of(ph, j) + t
                    acc_wait(ph, j, b)
                    act.copy(dst[:, t, j * NCOL:(j + 1) * NCOL], ACC[b][:]).then_inc(s, 1)
                    act.wait_ge(s, n + t + 1)
                    act.sem_inc(acc_free[b], 1)

            def head_squares():
                for t in range(NT):
                    act.activation(SQ[:, t], AQ[:, t], ACT.Square).then_inc(asq_ok, 1)

            def head_roots():
                act.wait_ge(arms_ok, 1)
                act.activation(ST2[:, 1], ST2[:, 0], ACT.Sqrt).then_inc(arms_ok, 1)

            def qt_out(n):
                act.wait_ge(aq_turned, n + 1)
                dst = KTT[:] if n == 0 else QT[:, 2 * n - 2:2 * n, :]
                act.copy(dst, SB[n % 4][0:64, :].rearrange("p (h t) -> p h t", h=2)).then_inc(qt_ok, 1)

            def softmax(h):
                act.wait_ge(ms_ok, h + 1)
                m = SMX[:, h % 2]
                act.activation(PA[:, h % 2, 0:P], PA[:, h % 2, 0:P], ACT.Exp, bias=m[:, 1, 0:1], accum_out=m[:, 2, 0:1])
                act.activation(PA[:, h % 2, P:], PA[:, h % 2, P:], ACT.Exp, bias=m[:, 1, 1:2], accum_out=m[:, 2, 1:2])
                act.activation(m[:, 3, :], m[:, 1, :], ACT.Exp, bias=NB[:, 128 + h:129 + h]).then_inc(pe_ok, 1)

            def pt_out(h):
                act.wait_ge(pt_done, h + 1)
                if h >= 2:
                    act.wait_ge(pv_done, h - 1)
                act.copy(PT[:, h % 2], SB[2 + h % 2][:, 0:384].rearrange("p (k q) -> p k q", k=3)).then_inc(pt_ok, 1)

            def hgrn_copy(g2):
                act.wait_ge(ob_done, g2 + 1)
                b = SB[SIDE_USER["hgrn", g2] % 2]
                act.copy(OB[:, :, g2 * 256:(g2 + 1) * 256].rearrange("p t (h d) -> p h t d", h=2),
                         b[:].rearrange("p (h t d) -> p h t d", h=2, t=NT))
                act.activation(b[:], b[:], ACT.Square).then_inc(obc_ok, 1)

            def hgrn_root():
                act.wait_ge(obr_ok, 1)
                act.activation(STB[:, 1], STB[:, 0], ACT.Sqrt).then_inc(obr_ok, 1)

            def gate2(ph, j, n):
                for t in range(NT):
                    b = 2 * pair_of(ph, j) + t
                    acc_wait(ph, j, b)
                    if n + t >= 2:
                        act.wait_ge(gate_free, n + t + 17)
                    act.activation(SG2[:, t], ACC[b][:], ACT.Silu).then_inc(gate_ok, 1)
                    act.wait_ge(gate_ok, n + t + 17)
                    act.sem_inc(acc_free[b], 1)

            def y_hi(x):
                act.wait_ge(y2_turned, x + 1)
                b = SB[SIDE_USER["turn", x] % 2][:].rearrange("p (k t) -> p k t", k=2)
                k0 = 8 + 2 * x if x < 4 else 2 * (x - 4)
                act.activation(HHI[:, 1, k0:k0 + 2, :], b, ACT.Copy,
                               scale=GNC[:, 0:1] if x < 4 else 1.0).then_inc(y2_hi, 1)

            def side2(b):
                if b == 8:
                    lower_bound()
                if b == 13:
                    log_add(0)
                if b == 29:
                    log_add(1)
                for hb, b0 in ((0, LEV0), (1, LEV1)):
                    if b0 + 2 <= b <= b0 + 16 and (b - b0) % 2 == 0:
                        level_exp(hb, (b - b0) // 2)
                    if b == b0 + 19:
                        att_wide(hb)
                if b == 59:
                    head_squares()
                if b == 60:
                    head_roots()
                if 66 <= b <= 68:
                    for n in range(3):
                        qt_out(3 * (b - 66) + n)
                for h in range(A_H):
                    if b == HEAD_BEAT + 2 * h + 7:
                        pt_out(h)
                    if b == HEAD_BEAT + 2 * h + 4:
                        softmax(h)
                for g2 in range(4):
                    if b == HGRN_BEAT + 2 * g2 + 4:
                        hgrn_copy(g2)
                if b == 84:
                    hgrn_root()
                for x in range(8):
                    if b == TURN_BEAT[x] + 4:
                        y_hi(x)

            act.wait_ge(nb_in, 64)
            split2 = lambda ph, cc, j, evict: split_steps(
                act, hi, ph, C2 + cc, j, {u: (lambda u=u: side2(8 * cc + u)) for u in range(3, 11)}, evict)
            for u in range(3):
                hi(C2 + 1, u, NCOL)
                side2(8 + u)
            bf_out(0)
            split2("BQ0", 1, 0, H(bq_out, 0))
            split2("BF1", 2, 0, H(bf_out, 1))
            split2("BQ1", 3, 0, H(bq_out, 1))
            split2("AK", 4, 0, ak_out)
            split2("AQ", 5, 0, H(tok_out, "AQ", 0, AQ, aq_ok, 2))
            split2("AQ", 6, 1, H(tok_out, "AQ", 1, AQ, aq_ok, 4))
            split2("BI", 7, 0, H(tok_out, "BI", 0, BI_, bi_ok, 0))
            split2("BI", 8, 1, H(tok_out, "BI", 1, BI_, bi_ok, 2))
            split2("BG", 9, 0, H(gate2, "BG", 0, 0))
            split2("BG", 10, 1, H(gate2, "BG", 1, 2))
            split2("AG", 11, 0, H(gate2, "AG", 0, 4))
            split2("AG", 12, 1, H(gate2, "AG", 1, 6))
            for j in range(4):
                split2("O2", 13 + j, j, nothing)


            C3 = chunk0["CQ0"]
            norm_in(1, 8)
            head_steps("odd", C3, NCOL, lambda x: half_hi(HHI[:, 0], "ln_odd_2", x, 3))

            def quad_out(q, x):
                ph, j = (("CQ0", "CK0", "CV0")[x], 0) if q == 0 else ("CR", 3 * (q - 1) + x)
                if q >= 2:
                    act.wait_ge(oc_done, 4 * q - 4)
                for y in range(2):
                    b = 2 * pair_of(ph, j) + y
                    acc_wait(ph, j, b)
                    if x < 2:
                        dst = (QF, KF)[x][:, q % 2, 2 * y:2 * y + 2, :].rearrange("p h t -> p (h t)")
                        o, s, n = act.activation(dst, ACC[b][:], ACT.Copy, scale=(C_D ** -0.5, 1.0)[x]), qk_ok, 4 * q + 2 * x + y
                    else:
                        o, s, n = act.copy(VF[:, q % 2, y, :], ACC[b][:]), cv_ok, 2 * q + y
                    o.then_inc(s, 1)
                    act.wait_ge(s, n + 1)
                    act.sem_inc(acc_free[b], 1)

            def soft_abs(h):
                act.wait_ge(z_done, h + 1)
                if h >= 2:
                    act.wait_ge(spm_ok, h - 1)
                t = TA[:, h % 2]
                seq(act.activation(t, SB[h % 2][:, 0:384], ACT.Abs))
                seq(act.activation(t, t, ACT.Exp, scale=-1.0))
                act.activation(t, t, ACT.Ln, bias=1.0).then_inc(ab_ok, 1)

            def stick_exp(h):
                act.wait_ge(sum_done, h + 1)
                if h >= 2:
                    act.wait_ge(oc_done, h - 1)
                act.activation(W3[:, h % 2].rearrange("p k q -> p (k q)"), SB[h % 2][:, 0:384], ACT.Exp).then_inc(w3_ok, 1)

            def gate3(j):
                for t in range(NT):
                    b = 2 * pair_of("CG", j) + t
                    acc_wait("CG", j, b)
                    if j:
                        act.wait_ge(gate_free, 2 * j + t + 25)
                    act.activation(SG3[:, t], ACC[b][:], ACT.Silu).then_inc(gate_ok, 1)
                    act.wait_ge(gate_ok, 2 * j + t + 25)
                    act.sem_inc(acc_free[b], 1)

            def y3_high(x):
                act.wait_ge(y2_turned, 8 + x + 1)
                act.copy(GHI[:, 2 * x:2 * x + 2, :].rearrange("p k t -> p (k t)"),
                         SB[2 + SIDE3_USER["turn", x] % 2][:]).then_inc(y2_hi, 1)

            def side3(b):
                for h in range(C_H):
                    if b == STICK_BEAT + 6 * h + 7:
                        stick_exp(h)
                    if b == STICK_BEAT + 6 * h + 4:
                        soft_abs(h)
                for x in range(8):
                    if b == TURN3_BEAT[x] + 4:
                        y3_high(x)

            split3 = lambda ph, cc, j, evict: split_steps(
                act, hi, ph, C3 + cc, j, {u: (lambda u=u: side3(8 * cc + u)) for u in range(3, 11)}, evict)
            for u in range(3):
                hi(C3 + 1, u, NCOL)
            quad_out(0, 0)
            split3("CK0", 1, 0, H(quad_out, 0, 1))
            split3("CV0", 2, 0, H(quad_out, 0, 2))
            for j in range(9):
                split3("CR", 3 + j, j, H(quad_out, 1 + j // 3, j % 3))
            for j in range(4):
                split3("CG", 12 + j, j, H(gate3, j))
            for j in range(4):
                split_steps(act, hi, "O3", C3 + 16 + j, j, {u: (lambda u=u: side3(8 * (16 + j) + u)) for u in range(3, 11)},
                            nothing, last=j == 3)

        @block.vector
        def _(dve):
            seq = Seq(dve, dve_seq)

            def lo(c, u, n):
                dve.wait_ge(hi_ready, c * UPC + (u + 1))
                dve.tensor_tensor(WLO[:, u % 4, :, 0:n], RAW[:, u % 4, :, 0:n],
                                  WHI[:, u % 4, :, 0:n].bitcast(F32), ALU.subtract).then_inc(lo_ready, 1)

            dve.sem_inc(gate_free, 2)
            dve.wait_ge(ssq_ok, 4)
            dve.tensor_scalar(STAT[:, 4:8], STAT[:, 0:4], 1.0 / D, EPS, ALU.mult, ALU.add).then_inc(std_ok, 1)
            dve.wait_ge(std_ok, 2)
            seq(dve.reciprocal(STAT[:, 12:16], STAT[:, 8:12]))
            for t in range(4):
                dve.tensor_scalar(XIN[:, t // 2, t % 2, :], XIN[:, t // 2, t % 2, :], STAT[:, 12 + t:13 + t], None,
                                  ALU.mult).then_inc(xn_ok, 1)
            with dve.Fori(0, 6) as i:
                for s in range(2):
                    dve.wait_ge(ada_used, i * 8 + (4 * s + 4))
                    dve.tensor_copy(ADR[:, bass.ds(i * 1024 + 512 * s, 512)], SB[1 + s][0:2, :]).then_inc(ada_ok, 1)
            dve.wait_ge(vec_ok, 2)
            dve.wait_ge(ada_done, 2)
            seq(dve.tensor_tensor(ADAV[:], SB[3][:, 0:96].rearrange("p (b s) -> p b s", s=2),
                                  VT[:, 1, 0:48].unsqueeze(2).to_broadcast([P, 48, 2]), ALU.add))
            for s in range(2):
                dve.tensor_copy(MOD[:, 2 + s, :], ADAV[:, 0:16, s])
                dve.scalar_tensor_tensor(MOD[:, s, :], ADAV[:, 16:32, s], 1.0, vec("g_pre", 0, 16), ALU.add, ALU.mult)
            dve.tensor_tensor(MOD[:, 4, :], ADAV[:, 32:48, 0], vec("g_post", 0, 16), ALU.mult).then_inc(mod_ok, 1)
            for u in range(3):
                lo(0, u, NCOL)
            for kt in range(KT):
                dve.wait_ge(hf_ok, 2 * kt + 2)
                f = HF[:, kt % 2, :].rearrange("p (a t) -> p a t", a=2)
                seq(dve.tensor_copy(HHI[:, :, kt, :], f))
                dve.tensor_tensor(HLO[:, :, kt, :], f, HHI[:, :, kt, :].bitcast(F32), ALU.subtract).then_inc(h_ok, 1)
                if kt in (4, 7, 10, 13, 15):
                    lo(0, 3 + (4, 7, 10, 13, 15).index(kt), NCOL)
            for u in range(3):
                lo(1, u, NCOL)

            def conv(n, blk, cb, ctx=True):
                dve.wait_ge(z_ok, n + 1)
                if isinstance(n, int) and n < 4:
                    pass
                else:
                    dve.wait_ge(t_done, n - 3) if not (isinstance(n, int) and n >= 24) else None
                w = lambda k: (VT[:, 2, bass.ds(blk + 32 * k, 1)] if k < 4 else VT[:, 3, bass.ds(blk, 1)])
                z, v = ZB[:, cb, :], CV[:, cb, :]
                end = 512 if ctx else SEQ
                seq(dve.tensor_scalar(v[:, 0:end], z[:, 0:end], w(2), VT[:, 1, bass.ds(blk + 48, 1)], ALU.mult, ALU.add))
                xr = lambda a: a[:, 0:SEQ].rearrange("p (r w) -> p r w", w=GRID_W)
                steps = []
                for k in (0, 1, 3, 4):
                    s = k - 2
                    a, b = max(0, -s), max(0, s)
                    for part in range(2 if ctx else 1):
                        zz, vv, wd = (xr(z), xr(v), GRID_W) if part == 0 else (z[:, SEQ:], v[:, SEQ:], SEQ)
                        m = wd - abs(s)
                        zi, vo = (zz[:, :, b:b + m], vv[:, :, a:a + m]) if part == 0 else (zz[:, b:b + m], vv[:, a:a + m])
                        steps.append((vo, zi, w(k)))
                for x, (vo, zi, wk) in enumerate(steps):
                    ins_ = dve.scalar_tensor_tensor(vo, zi, wk, vo, ALU.mult, ALU.add)
                    if x == len(steps) - 1:
                        ins_.then_inc(conv_ok, 1)
                    else:
                        seq(ins_)

            def b_out(n, cb):
                dve.wait_ge(t_done, n + 1)
                dve.tensor_copy(BK[:, :, n * P:(n + 1) * P], SB[cb][:, 0:256].rearrange("p (t n) -> p t n", t=NT)).then_inc(t_free, 1)

            def x_out(k, cb):
                n = k * 4 + (8 + cb)
                dve.wait_ge(t_done, n + 1)
                s = SB[cb][:].rearrange("p (t n) -> p t n", t=4)
                dve.tensor_copy(XH[:, :, bass.ds(k * 512 + cb * P, P)], s[:, 0:2])
                dve.tensor_copy(XC[:, :, cb * P:(cb + 1) * P], s[:, 2:4]).then_inc(t_free, 1)

            def weigh(k, first=False):
                dve.wait_ge(t_free, k * 4 + 12)
                if not first:
                    dve.wait_ge(st_done, k * 2)
                for d in range(2):
                    for t in range(NT):
                        o = dve.tensor_tensor(XW[:, d, t, :].rearrange("p (h e) -> p h e", e=HD),
                                              XC[:, t, :].rearrange("p (h e) -> p h e", e=HD),
                                              WCX[:, t, bass.ds(k * 8 + d * 32, 8)].unsqueeze(2).to_broadcast([P, 8, HD]),
                                              ALU.mult)
                    o.then_inc(xw_ok, 1)

            def dt_bias():
                dve.wait_ge(dt_turned, 1)
                dve.wait_ge(bc_in, 48)
                dve.tensor_tensor(AW[:, 0], SB[3][:, 0:256].rearrange("p (t h) -> p t h", t=4),
                                  BCS[:, 0:64].unsqueeze(1).to_broadcast([P, 4, 64]), ALU.add).then_inc(dtr_ok, 1)
                dve.wait_ge(dtr_ok, 1)
                dve.scalar_tensor_tensor(AW[:, 1], AW[:, 0], -1.0, AW[:, 0], ALU.mult, ALU.max).then_inc(dtr_ok, 1)

            def dt_soft():
                dve.wait_ge(dtl_ok, 1)
                seq(dve.scalar_tensor_tensor(DTV[:], AW[:, 0], 0.0, AW[:, 1], ALU.max, ALU.add))
                seq(dve.tensor_scalar(AW[:, 2, 0], AW[:, 2, 0], -1.0, None, ALU.mult))
                dve.tensor_tensor(AW[:, 3], DTV[:], AW[:, 2, 0].unsqueeze(1).to_broadcast([P, 4, 64]), ALU.mult).then_inc(a_ok, 1)

            def cum_in():
                dve.wait_ge(cums_ok, 5)
                dve.tensor_tensor(ART[0:32, 1, :], SB[3][0:32, 0:256], ART[0:32, 0, :].bitcast(F32), ALU.subtract)
                dve.tensor_tensor(ART[32:64, 1, :], SB[3][32:64, 256:512], ART[32:64, 0, :].bitcast(F32), ALU.subtract)
                dve.tensor_tensor(WCX[:], WCX[:], DTV[:, 2:4], ALU.mult).then_inc(cums_ok, 1)
                dve.wait_ge(cums_ok, 6)

            H = lambda f, *a: (lambda: f(*a))
            both = lambda *fs: (lambda: [f() for f in fs])
            split_steps(dve, lo, "DT", 1, 0, {}, lambda: None)
            mid = {3 + cb: H(conv, cb, 16 + cb, cb) for cb in range(4)}
            mid[3] = both(dt_bias, mid[3])
            for cb in range(4):
                f = H(b_out, cb, cb)
                mid[5 + cb] = both(mid[5 + cb], f) if 5 + cb in mid else f
            split_steps(dve, lo, "B1", 2, 0, mid, lambda: None)
            X0, C0 = chunk0["X"], chunk0["C"]
            mid = {3 + cb: H(conv, 4 + cb, 20 + cb, cb) for cb in range(4)}
            mid[4] = both(mid[4], dt_soft)
            for cb in range(4):
                f = H(b_out, 4 + cb, cb)
                mid[5 + cb] = both(mid[5 + cb], f) if 5 + cb in mid else f
            mid[9] = cum_in
            split_steps(dve, lo, "X", X0, 0, mid, lambda: None)

            def conv_mid(n, k):
                mid = {3 + cb: H(conv, n + cb, k * 4 + cb, cb) for cb in range(4)}
                for cb in range(4):
                    f = H(x_out, k, cb)
                    mid[5 + cb] = both(mid[5 + cb], f) if 5 + cb in mid else f
                return mid

            mid = conv_mid(8, 0)
            mid[9] = H(weigh, 0, True)
            split_steps(dve, lo, "X", X0 + 1, 1, mid, lambda: None)
            with dve.Fori(0, 2) as i:
                seq.enter(i, 32)
                mid = conv_mid(i * 4 + 12, i + 1)
                mid[9] = H(weigh, i + 1)
                split_steps(dve, lo, "X", i + (X0 + 2), 0, mid, lambda: None)
                seq.leave(2)
            mid = conv_mid(20, 3)
            mid[9] = H(weigh, 3)
            split_steps(dve, lo, "C", C0, 0, mid, lambda: None)
            nothing = lambda: None
            split_steps(dve, lo, "C", C0 + 1, 1, {3 + cb: H(conv, 24 + cb, 24 + cb, cb, False) for cb in range(4)}, nothing)

            def ws_out(x):
                dve.wait_ge(ws_turned, x + 1)
                dve.wait_ge(silu_ok, 32)
                dve.tensor_copy(WST[:, 4 * x:4 * x + 4, :], SB[x][:].rearrange("p (g q) -> p g q", g=4)).then_inc(ws_ok, 1)

            def mean_root(ready, n, col, c, s):
                dve.wait_ge(ready, n)
                seq(dve.tensor_reduce(STAT[:, c:c + 2], STAT[:, col:col + 8].rearrange("p (t q) -> p t q", t=NT), AX.X, ALU.add))
                dve.tensor_scalar(STAT[:, c:c + 2], STAT[:, c:c + 2], 1.0 / D, EPS, ALU.mult, ALU.add).then_inc(s, 1)

            def invert(s, c):
                dve.wait_ge(s, 2)
                seq(dve.reciprocal(STAT[:, c + 2:c + 4], STAT[:, c + 2:c + 4]))

            def v_norm(q):
                t, h = q // 2, q % 2
                s = slice(h * 1024, (h + 1) * 1024)
                dve.wait_ge(gv_in, 16)
                dve.scalar_tensor_tensor(V[:, t, s], V[:, t, s], STAT[:, 26 + t:27 + t], GV[:, s], ALU.mult,
                                         ALU.mult).then_inc(vn_ok, 1)

            def u_out(j, i=0):
                for t in range(NT):
                    b = 2 * (j % 2) + t
                    dve.wait_ge(acc_done[b], before["U", j][b] + 1)
                    if j == 0:
                        dve.wait_ge(sg_ok, 2)
                    dve.wait_ge(sg_ok, min(8, 2 * j + 2))
                    tt = T[:, t, j * NCOL:(j + 1) * NCOL]
                    seq(dve.tensor_tensor(tt, ACC[b][:], tt, ALU.mult))
                    dve.sem_inc(acc_free[b], 1)

            def off_out(g, d):
                dve.wait_ge(yo_done, g * 2 + d + 1)
                if d == 0:
                    dve.wait_ge(yd_ok, g + 1)
                s = SB[3][:].rearrange("p (t r e) -> p t r e", t=NT, r=RH)
                ea = ACS[:, 2, :, bass.ds(g * 4 + 32 * d, 4)].unsqueeze(3).to_broadcast([P, NT, RH, HD])
                dve.tensor_tensor(YT[:].rearrange("p t (r e) -> p t r e", r=RH), s, ea, ALU.mult).then_inc(yo_used, 1)
                dve.wait_ge(yo_used, g * 2 + d + 1)
                y = Y[:, :, bass.ds(g * 256, 256)]
                seq(dve.tensor_tensor(y, y, YT[:], ALU.add))

            def heads(g, r):
                dve.wait_ge(e_ok, g * 4 + r + 1)
                if not (isinstance(g, int) and g * 4 + r < 2):
                    dve.wait_ge(y_done, g * 4 + r - 1)
                e, m = EX[:, r % 2], MM[:, r % 2]
                dt = lambda d, k: DTV[:, k, bass.ds(g * 4 + (32 * d + r), 1)]
                dve.tensor_scalar(m[:, 0, :], e[:, 0:256], dt(0, 0), None, ALU.mult)
                seq(dve.tensor_scalar(m[:, 1, :], e[:, 512:768], dt(1, 1), None, ALU.mult))
                dve.scalar_tensor_tensor(m[:, 0, 0:P], e[:, 384:512], dt(1, 0), m[:, 0, 0:P], ALU.mult, ALU.add)
                seq(dve.scalar_tensor_tensor(m[:, 1, P:], e[:, 256:384], dt(0, 1), m[:, 1, P:], ALU.mult, ALU.add))
                if r == 0:
                    dve.wait_ge(cbs_ok, g + 1)
                dve.tensor_tensor(m, m, CBS[:], ALU.mult).then_inc(m_ok, 1)

            def y_sum(g):
                dve.wait_ge(y_done, g * 4 + 4)
                y = Y[:, :, bass.ds(g * 256, 256)]
                dve.tensor_tensor(y, SB[2][:].rearrange("p (t e) -> p t e", t=NT), y, ALU.add).then_inc(y_ok, 1)

            def ssd_mid(g):
                return {3: lambda: (off_out(g, 0), off_out(g, 1)), 4: H(heads, g, 0), 5: H(heads, g, 1),
                        6: H(heads, g, 2), 7: H(heads, g, 3), 8: H(y_sum, g)}

            def gated(dst, ph, j, n, s):
                if ph == "S":
                    dve.wait_ge(y_ok, min(8, 2 * j + 2))
                for t in range(NT):
                    dve.wait_ge(gate_ok, n + t + 1)
                    x = dst[:, t, (bass.ds(j * NCOL, NCOL))]
                    dve.tensor_tensor(x, x, SG[:, t], ALU.mult).then_inc(gate_free, 1)
                if s is not None:
                    dve.wait_ge(gate_free, n + 4)
                    dve.sem_inc(s, 2)

            cV, cU, cM, cS, cO = (chunk0[n] for n in ("V", "U", "M", "S", "O1"))
            split_steps(dve, lo, "V", cV, 0, {3 + cb: H(conv, 28 + cb, 28 + cb, cb, False) for cb in range(4)}, nothing)
            split_steps(dve, lo, "V", cV + 1, 1, {3 + x: H(ws_out, x) for x in range(4)}, nothing)
            split_steps(dve, lo, "V", cV + 2, 2, {}, nothing)
            split_steps(dve, lo, "V", cV + 3, 3, {}, nothing)
            mean = H(mean_root, v_ok, 8, 16, 24, vstd_ok)
            split_steps(dve, lo, "U", cU, 0, {3: both(mean, H(invert, vstd_ok, 24), H(v_norm, 0)), 4: H(v_norm, 1),
                                              5: H(v_norm, 2), 6: H(v_norm, 3)}, H(u_out, 0))
            split_steps(dve, lo, "U", cU + 1, 1, {}, H(u_out, 1))
            split_steps(dve, lo, "U", cU + 2, 2, ssd_mid(0), H(u_out, 2))
            split_steps(dve, lo, "U", cU + 3, 3, ssd_mid(1), H(u_out, 3))
            with dve.Fori(0, 2) as i:
                seq.enter(i, 20)
                for j in range(2):
                    split_steps(dve, lo, "M", i * 2 + (cM + j), j, ssd_mid(i * 2 + (2 + j)),
                                H(gated, T, "M", i * 2 + j, i * 4 + 2 * j, t_ok))
                seq.leave(2)
            split_steps(dve, lo, "S", cS, 0, ssd_mid(6), H(gated, Y, "S", 0, 8, yg_ok))
            split_steps(dve, lo, "S", cS + 1, 1, ssd_mid(7), H(gated, Y, "S", 1, 10, yg_ok))

            def t_norm():
                mean_root(tsq_ok, 8, 32, 40, tstd_ok)
                invert(tstd_ok, 40)
                for t in range(NT):
                    dve.tensor_scalar(T[:, t], T[:, t], STAT[:, 42 + t:43 + t], None, ALU.mult).then_inc(tn_ok, 1)

            def half_lo(dst, hi_t, gname, x, k0):
                for k in range(2):
                    kt = 2 * x + k
                    dve.wait_ge(h_hi, 16 * k0 + 2 * x + 2)
                    dve.scalar_tensor_tensor(dst[:, kt, :], SB[x % 4][:, k * SEQ:(k + 1) * SEQ], vec(gname, kt),
                                             hi_t[:, kt, :].bitcast(F32), ALU.mult, ALU.subtract).then_inc(h_lo, 1)

            split_steps(dve, lo, "S", cS + 2, 2, {5: t_norm}, H(gated, Y, "S", 2, 12, yg_ok))
            mid = {u: H(half_lo, GLO, GHI, "g_mlp", u - 3, 0) for u in range(3, 11)}
            split_steps(dve, lo, "S", cS + 3, 3, mid, H(gated, Y, "S", 3, 14, yg_ok))
            mean_root(ysq_ok, 8, 44, 52, ystd_ok)
            invert(ystd_ok, 52)
            for t in range(NT):
                dve.tensor_scalar(Y[:, t], Y[:, t], STAT[:, 54 + t:55 + t], None, ALU.mult).then_inc(yn_ok, 1)
            for u in range(3, 8):
                lo(cO, u, NCOL)
            for x in range(8):
                half_lo(HLO[:, 0], HHI[:, 0], "g_ssd", x, 1)
            for u in range(3):
                lo(cO + 1, u, NCOL)

            def o_part(r):
                for t in range(NT):
                    b = 2 * (r % 2) + t
                    dve.wait_ge(acc_done[b], before["O1", 2 * r + 1][b] + 1)
                    dve.wait_ge(gg_ok, 4)
                    dve.wait_ge(osq_ok, 2 * r + t + 1)
                    s = slice(r * NCOL, (r + 1) * NCOL)
                    dve.tensor_tensor(O[:, t, s], ACC[b][:], GG[:, s], ALU.mult).then_inc(o_ok, 1)
                    dve.wait_ge(o_ok, 2 * r + t + 1)
                    dve.sem_inc(acc_free[b], 1)

            for r in range(4):
                if r:
                    split_steps(dve, lo, "O1", cO + 2 * r, 2 * r, {}, nothing)
                split_steps(dve, lo, "O1", cO + 2 * r + 1, 2 * r + 1, {}, H(o_part, r))
            mean_root(osq_ok, 8, 16, 56, ostd_ok)
            invert(ostd_ok, 56)
            dve.wait_ge(xr_in, 16)
            for t in range(NT):
                dve.scalar_tensor_tensor(X1[:, t], O[:, t], STAT[:, 58 + t:59 + t], XR[:, t], ALU.mult, ALU.add).then_inc(x_ok, 1)

            def norm_out(L):
                dve.wait_ge(nsq_ok, 2 * L + 2)
                dve.tensor_scalar(ST3[:, 2:4], ST3[:, 0:2], 1.0 / D, EPS, ALU.mult, ALU.add).then_inc(nrt_ok, 1)
                dve.wait_ge(nrt_ok, 2 * L + 2)
                seq(dve.reciprocal(ST3[:, 6:8], ST3[:, 4:6]))
                for t in range(NT):
                    dve.tensor_scalar(XN[:, t], X1[:, t], ST3[:, 6 + t:7 + t], None, ALU.mult).then_inc(nxn_ok, 1)

            def head_steps(c, n, half):
                lo(c, 3, n)
                for x in range(4):
                    half(x)
                for u in range(4, 8):
                    half(u)
                    lo(c, u, n)

            C2 = chunk0["BF0"]
            norm_out(0)
            head_steps(C2, NCOL, lambda x: half_lo(HLO[:, 0], HHI[:, 0], "ln_even_2", x, 2))

            def lower_bound_exp():
                lb = vec("lower_bounds_2", 0, 8)
                dve.tensor_tensor(LBC[:, 5], lb, lb, ALU.subtract).then_inc(lb_sem, 1)

            def lower_bound():
                dve.wait_ge(lb_sem, 2)
                seq(dve.reciprocal(LBC[:, 0], LBC[:, 5]))
                seq(dve.tensor_tensor(LBC[:, 1], LBC[:, 0], LBC[:, 5], ALU.mult))
                seq(dve.tensor_tensor(LBC[:, 0], LBC[:, 1], LBC[:, 1], ALU.subtract))
                seq(dve.tensor_scalar(LBC[:, 1], LBC[:, 0], -1.0, 1.0, ALU.mult, ALU.add))
                seq(dve.tensor_scalar(LBC[:, 5], LBC[:, 0], LB_FLOOR, None, ALU.max))
                dve.tensor_tensor(LBC[:, 2], LBC[:, 5], LBC[:, 0], ALU.subtract).then_inc(lb_sem, 1)
                dve.wait_ge(lb_sem, 4)
                seq(dve.tensor_scalar(LBC[:, 4], LBC[:, 4], -64.0 * float(np.log(2.0)), None, ALU.add))

            def bf_steps(hb):
                dve.wait_ge(p1_ok, hb + 1)
                seq(dve.scalar_tensor_tensor(P1[:], P1[:], 0.0, VV[:, hb], ALU.min, ALU.subtract))
                cst = lambda r, h: LBC[:, r, 4 * hb + h:4 * hb + h + 1]
                for h in range(4):
                    o = dve.tensor_scalar(KI[:, hb, h], KI[:, hb, h], cst(1, h), cst(2, h), ALU.mult, ALU.subtract)
                o.then_inc(ki_ok, 1)
                for h in range(4):
                    o = dve.tensor_scalar(P1[:, h], P1[:, h], cst(3, h), None, ALU.add)
                seq(o)
                for h in range(4):
                    dve.tensor_scalar(U_[:, hb, h], P1[:, h], cst(4, h), None, ALU.max)
                    o = dve.tensor_scalar(P1[:, h], P1[:, h], cst(4, h), None, ALU.subtract)
                seq(o)
                dve.scalar_tensor_tensor(P1[:], P1[:], -1.0, P1[:], ALU.mult, ALU.max).then_inc(la_ok, 1)
                dve.memset(VV[:, hb], 0.0)

            def log_f(hb):
                dve.wait_ge(lx_ok, hb + 1)
                dve.tensor_tensor(U_[:, hb], U_[:, hb], P1[:], ALU.add).then_inc(logf_ok, 1)

            def level_mult(hb, l):
                dve.wait_ge(we_ok, 16 * hb + 2 * l)
                if l == 1:
                    dve.wait_ge(bq_ok, hb + 1)
                for src, up in ((BQ_, 1), (KI, 0)):
                    w = level(WL[:, l % 2], l, up)
                    o = dve.tensor_tensor(w, w, level(src[:, hb], l, up), ALU.mult)
                o.then_inc(wl_ok, 1)

            def pick(hb, l):
                n = hb * 9 + l
                dve.wait_ge(at_done, n + 1)
                if n == 0:
                    dve.wait_ge(hm_in, 16)
                for y in range(2):
                    b = SB[2 * (n % 2) + y][:].rearrange("p (a q) -> p a q", a=4)
                    a = ATT[:, hb, 2 * y:2 * y + 2].rearrange("p h k q -> p (h k) q")
                    m = HM[:, l, :].unsqueeze(1).to_broadcast([P, 4, P])
                    if l == 0:
                        seq(dve.tensor_tensor(a, b, m, ALU.mult))
                    else:
                        seq(dve.copy_predicated(a, m.bitcast(mybir.dt.int32), b))
                dve.sem_inc(at_ok, 1)

            def head_means():
                dve.wait_ge(asq_ok, 2)
                seq(dve.tensor_reduce(ST2[:, 1], SQ[:].rearrange("p t (h e) -> p t h e", e=A_D), AX.X, ALU.add))
                dve.tensor_scalar(ST2[:, 0], ST2[:, 1], 1.0 / A_D, EPS, ALU.mult, ALU.add).then_inc(arms_ok, 1)

            def head_norm():
                dve.wait_ge(arms_ok, 2)
                dve.wait_ge(nb_in, 64)
                seq(dve.reciprocal(ST2[:, 0], ST2[:, 1]))
                seq(dve.tensor_scalar(ST2[:, 0, :, 0:16], ST2[:, 0, :, 0:16], A_D ** -0.5, None, ALU.mult))
                for t in range(NT):
                    x = AQ[:, t].rearrange("p (h e) -> p h e", e=A_D)
                    seq(dve.tensor_tensor(x, x, ST2[:, 0, t].unsqueeze(2).to_broadcast([P, 18, A_D]), ALU.mult))
                    dve.tensor_tensor(x[:, 0:16], x[:, 0:16], NB[:, 0:64].unsqueeze(1).to_broadcast([P, 16, A_D]), ALU.mult)
                    seq(dve.tensor_tensor(x[:, 16:18], x[:, 16:18], NB[:, 64:128].unsqueeze(1).to_broadcast([P, 2, A_D]), ALU.mult))

            def rope(t):
                x = AQ[:, t].rearrange("p (h e) -> p h e", e=A_D)
                x1, x2 = x[:, :, 0:32], x[:, :, 32:64]
                c = con("cos")[:, t * 32:(t + 1) * 32].unsqueeze(1).to_broadcast([P, 18, 32])
                s = con("sin")[:, t * 32:(t + 1) * 32].unsqueeze(1).to_broadcast([P, 18, 32])
                r = [RT[:, k].rearrange("p (h e) -> p h e", e=32) for k in range(4)]
                dve.tensor_tensor(r[0], x1, c, ALU.mult)
                dve.tensor_tensor(r[1], x2, s, ALU.mult)
                dve.tensor_tensor(r[2], x2, c, ALU.mult)
                seq(dve.tensor_tensor(r[3], x1, s, ALU.mult))
                dve.tensor_tensor(x1, r[0], r[1], ALU.subtract)
                o = dve.tensor_tensor(x2, r[2], r[3], ALU.add)
                if t == 0:
                    seq(o)
                else:
                    o.then_inc(rope_ok, 1)

            def mask_max(h):
                dve.wait_ge(sc_done, h + 1)
                if h >= 2:
                    dve.wait_ge(pt_done, h - 1)
                b, m, p = SB[SIDE_USER["scores", h] % 2], SMX[:, h % 2], PA[:, h % 2]
                dve.tensor_tensor(p[:, 0:256], b[:, 0:256], CON[:, CAT["band0"]:CAT["band0"] + 256], ALU.add)
                seq(dve.tensor_tensor(p[:, 256:], b[:, 256:384], con("band0"), ALU.add))
                dve.sem_inc(side_free, 1)
                dve.tensor_reduce(m[:, 0, 0:1], p[:, 0:P], AX.X, ALU.max)
                seq(dve.tensor_reduce(m[:, 0, 1:2], p[:, P:], AX.X, ALU.max))
                dve.tensor_scalar(m[:, 1], m[:, 0], NB[:, 128 + h:129 + h], -1.0, ALU.max, ALU.mult).then_inc(ms_ok, 1)

            def over_sum(h):
                dve.wait_ge(pe_ok, h + 1)
                m = SMX[:, h % 2]
                seq(dve.tensor_tensor(m[:, 4], m[:, 2], m[:, 3], ALU.add))
                seq(dve.reciprocal(m[:, 5], m[:, 4]))

            def weigh_out(h):
                dve.wait_ge(pv_done, h + 1)
                dve.tensor_tensor(YA[:, :, h * A_D:(h + 1) * A_D], SB[2 + h % 2][:, 384:512].rearrange("p (t e) -> p t e", t=NT),
                                  SMX[:, h % 2, 5].unsqueeze(2).to_broadcast([P, NT, A_D]), ALU.mult).then_inc(ya_ok, 1)

            def hgrn_sums(g2):
                dve.wait_ge(obc_ok, g2 + 1)
                b = SB[SIDE_USER["hgrn", g2] % 2]
                seq(dve.tensor_reduce(STB[:, 1, :, 2 * g2:2 * g2 + 2].rearrange("p t h -> p h t"),
                                      b[:].rearrange("p (h t d) -> p h t d", h=2, t=NT), AX.X, ALU.add))
                dve.sem_inc(side_free, 1)

            def hgrn_mean():
                dve.tensor_scalar(STB[:, 0], STB[:, 1], 1.0 / B_D, EPS, ALU.mult, ALU.add).then_inc(obr_ok, 1)

            def hgrn_norm():
                dve.wait_ge(obr_ok, 2)
                seq(dve.reciprocal(STB[:, 0], STB[:, 1]))
                dve.wait_ge(gate_free, 22)
                for t in range(NT):
                    x = OB[:, t].rearrange("p (h d) -> p h d", h=B_H)
                    o = dve.tensor_tensor(x, x, STB[:, 0, t].unsqueeze(2).to_broadcast([P, B_H, B_D]), ALU.mult)
                o.then_inc(yb_ok, 1)

            def gated2(dst, j, n):
                for t in range(NT):
                    dve.wait_ge(gate_ok, n + t + 17)
                    x = dst[:, t, j * NCOL:(j + 1) * NCOL]
                    dve.tensor_tensor(x, x, SG2[:, t], ALU.mult).then_inc(gate_free, 1)

            def bg_out(j):
                dve.wait_ge(obc_ok, 2 * j + 2)
                gated2(OB, j, 2 * j)

            def ag_out(j):
                dve.wait_ge(ya_ok, 16 if j else 8)
                gated2(YA, j, 4 + 2 * j)

            def y_lo(x):
                dve.wait_ge(y2_hi, x + 1)
                b = SB[SIDE_USER["turn", x] % 2][:].rearrange("p (k t) -> p (k t)", k=2)
                k0 = 8 + 2 * x if x < 4 else 2 * (x - 4)
                flat = lambda T_: T_[:, 1, k0:k0 + 2, :].rearrange("p k t -> p (k t)")
                dve.scalar_tensor_tensor(flat(HLO), b, GNC[:, 0:1] if x < 4 else 1.0,
                                         flat(HHI).bitcast(F32), ALU.mult, ALU.subtract).then_inc(y2_lo, 2)
                dve.wait_ge(y2_lo, 2 * x + 2)
                dve.sem_inc(side_free, 1)

            def side2(b):
                if b == 11:
                    bf_steps(0)
                if b == 13:
                    log_f(0)
                if b == 27:
                    bf_steps(1)
                if b == 29:
                    log_f(1)
                for hb, b0 in ((0, LEV0), (1, LEV1)):
                    if b0 + 2 <= b <= b0 + 16 and (b - b0) % 2 == 0:
                        level_mult(hb, (b - b0) // 2)
                    if b0 + 3 <= b <= b0 + 17 and (b - b0) % 2:
                        pick(hb, (b - b0 - 3) // 2)
                if b == 59:
                    head_means()
                if b == 60:
                    head_norm()
                if b in (61, 62):
                    rope(b - 61)
                for h in range(A_H):
                    if b == HEAD_BEAT + 2 * h + 10:
                        weigh_out(h)
                    if b == HEAD_BEAT + 2 * h + 6:
                        over_sum(h)
                    if b == HEAD_BEAT + 2 * h + 4:
                        mask_max(h)
                for g2 in range(4):
                    if b == HGRN_BEAT + 2 * g2 + 4:
                        hgrn_sums(g2)
                if b == 84:
                    hgrn_mean()
                if b == 91:
                    hgrn_norm()
                for x in range(8):
                    if b == TURN_BEAT[x] + 4:
                        y_lo(x)

            def residual(j):
                for t in range(NT):
                    b = 2 * pair_of("O2", j) + t
                    dve.wait_ge(acc_done[b], before["O2", j][b] + 1)
                    s = slice(j * NCOL, (j + 1) * NCOL)
                    dve.tensor_tensor(X1[:, t, s], ACC[b][:], X1[:, t, s], ALU.add).then_inc(x_ok, 1)
                    dve.wait_ge(x_ok, 2 + 2 * j + t + 1)
                    dve.sem_inc(acc_free[b], 1)

            split2 = lambda ph, cc, j, evict: split_steps(
                dve, lo, ph, C2 + cc, j, {u: (lambda u=u: side2(8 * cc + u)) for u in range(3, 11)}, evict)
            lower_bound_exp()
            for u in range(3):
                lo(C2 + 1, u, NCOL)
                if u == 0:
                    lower_bound()
            split2("BQ0", 1, 0, nothing)
            split2("BF1", 2, 0, nothing)
            split2("BQ1", 3, 0, nothing)
            split2("AK", 4, 0, nothing)
            split2("AQ", 5, 0, nothing)
            split2("AQ", 6, 1, nothing)
            split2("BI", 7, 0, nothing)
            split2("BI", 8, 1, nothing)
            split2("BG", 9, 0, H(bg_out, 0))
            split2("BG", 10, 1, H(bg_out, 1))
            split2("AG", 11, 0, H(ag_out, 0))
            split2("AG", 12, 1, H(ag_out, 1))
            for j in range(4):
                split2("O2", 13 + j, j, H(residual, j))


            C3 = chunk0["CQ0"]
            norm_out(1)
            head_steps(C3, NCOL, lambda x: half_lo(HLO[:, 0], HHI[:, 0], "ln_odd_2", x, 3))

            def softplus(h):
                dve.wait_ge(ab_ok, h + 1)
                if h >= 2:
                    dve.wait_ge(sum_done, h - 1)
                s = SPM[:, h % 2]
                dve.scalar_tensor_tensor(s.rearrange("p k q -> p (k q)"), SB[h % 2][:, 0:384], 0.0, TA[:, h % 2],
                                         ALU.max, ALU.add).then_inc(spm_ok, 1)

            def oc_copy(h):
                dve.wait_ge(oc_done, h + 1)
                dve.tensor_copy(OC[:, :, h * P:(h + 1) * P],
                                SB[2 + SIDE3_USER["out", h] % 2][:, 0:256].rearrange("p (t d) -> p t d", t=NT)).then_inc(oc_ok, 1)
                dve.wait_ge(oc_ok, h + 1)
                dve.sem_inc(side_free, 1)

            def gated3(j):
                for t in range(NT):
                    dve.wait_ge(gate_ok, 2 * j + t + 25)
                    x = OC[:, t, j * NCOL:(j + 1) * NCOL]
                    dve.tensor_tensor(x, x, SG3[:, t], ALU.mult).then_inc(gate_free, 1)

            def y3_low(x):
                dve.wait_ge(y2_hi, 8 + x + 1)
                flat = lambda T_: T_[:, 2 * x:2 * x + 2, :].rearrange("p k t -> p (k t)")
                dve.tensor_tensor(flat(GLO), SB[2 + SIDE3_USER["turn", x] % 2][:], flat(GHI).bitcast(F32),
                                  ALU.subtract).then_inc(y2_lo, 1)
                dve.wait_ge(y2_lo, 16 + x + 1)
                dve.sem_inc(side_free, 1)

            def side3(b):
                for h in range(C_H):
                    if b == STICK_BEAT + 6 * h + 10:
                        oc_copy(h)
                    if b == STICK_BEAT + 6 * h + 4:
                        softplus(h)
                for x in range(8):
                    if b == TURN3_BEAT[x] + 4:
                        y3_low(x)

            def result(j):
                for t in range(NT):
                    b = 2 * pair_of("O3", j) + t
                    dve.wait_ge(acc_done[b], before["O3", j][b] + 1)
                    s = slice(j * NCOL, (j + 1) * NCOL)
                    dve.tensor_tensor(X1[:, t, s], ACC[b][:], X1[:, t, s], ALU.add).then_inc(x_ok, 1)
                    dve.wait_ge(x_ok, 10 + 2 * j + t + 1)
                    dve.sem_inc(acc_free[b], 1)

            split3 = lambda ph, cc, j, evict, last=False: split_steps(
                dve, lo, ph, C3 + cc, j, {u: (lambda u=u: side3(8 * cc + u)) for u in range(3, 11)}, evict, last)
            for u in range(3):
                lo(C3 + 1, u, NCOL)
            split3("CK0", 1, 0, nothing)
            split3("CV0", 2, 0, nothing)
            for j in range(9):
                split3("CR", 3 + j, j, nothing)
            for j in range(4):
                split3("CG", 12 + j, j, H(gated3, j))
            for j in range(4):
                split3("O3", 16 + j, j, H(result, j), last=j == 3)

        @block.gpsimd
        def _(pool):
            pool.wait_ge(t_free, 8)
            for k in range(1):
                pool.tensor_copy(BG[:], BK[:, :, 0:256].rearrange("p t (g n) -> p t g n", g=2)).then_inc(bg_ok, 1)
            with pool.Fori(1, 4) as k:
                pool.wait_ge(st_done, k * 2)
                pool.tensor_copy(BG[:].rearrange("p t g n -> p t (g n)"), BK[:, :, bass.ds(k * 256, 256)]).then_inc(bg_ok, 1)
            pool.wait_ge(sg_ok, 8)

            def group(g, first=False):
                if not first:
                    pool.wait_ge(y_ok, g)
                pool.tensor_copy(GB[:, 0, :], BT[:, bass.ds(g, 1), :])
                pool.tensor_copy(GB[:, 1, :], CT[:, bass.ds(g, 1), :])
                ident = CON[0:64, 0:64].rearrange("p (d h) -> p d h", d=2)
                pool.tensor_copy(SEL[:], ident[:, :, bass.ds(g * 4, 4)]).then_inc(gb_ok, 1)
                pool.tensor_tensor(Y[:, :, bass.ds(g * 256, 256)].rearrange("p t (r e) -> p t r e", r=RH),
                                   XH[:, :, bass.ds(g * 256, 256)].rearrange("p t (r e) -> p t r e", r=RH),
                                   BCS[:, bass.ds(g * 4 + 128, 4)].unsqueeze(1).unsqueeze(3).to_broadcast([P, NT, RH, HD]),
                                   ALU.mult).then_inc(yd_ok, 1)

            pool.wait_ge(silu_ok, 32)
            group(0, True)
            with pool.Fori(1, 8) as g:
                group(g)

            def sums_on(hb, l):
                pool.wait_ge(we_ok, 16 * hb + 2 * l)
                s = 2 ** (l - 1)
                n = 4 * SEQ // (2 * s)
                u = U_[:, hb].rearrange("p h (n s) -> p (h n) s", s=2 * s)
                v = VV[:, hb].rearrange("p h (n s) -> p (h n) s", s=2 * s)
                pool_seq(pool.tensor_tensor(v[:, :, 0:s], v[:, :, 0:s], u[:, :, 2 * s - 1:2 * s].to_broadcast([P, n, s]), ALU.add))
                pool.tensor_tensor(u[:, :, s:], u[:, :, s:], u[:, :, s - 1:s].to_broadcast([P, n, s]), ALU.add).then_inc(uv_ok, 1)

            pool_seq = Seq(pool, pool_step)
            for hb in range(2):
                pool.wait_ge(logf_ok, hb + 1)
                for l in range(1, 8):
                    sums_on(hb, l)

            pool.wait_ge(h_turned, 32)
            pool.tensor_scalar(NEG3[:, 0], con("ge"), -1.0, None, ALU.mult)
            pool.tensor_scalar(NEG3[:, 1], con("one"), -1.0, None, ALU.mult)
            pool.tensor_scalar(NM3[:], con("ge"), -1e30, None, ALU.mult).then_inc(n3_ok, 1)


_INS = ("x", "c", "ctx", "c_ctx", "w_ada", "b_ada", "g_pre", "g_post", "w_in", "conv_w", "conv_b", "dt_bias",
        "a_log", "d_skip", "g_ssd", "g_v", "w_s", "b_s", "g_mlp", "w_out", "ln_even_2", "w_in_even_2",
        "q_norm_a_2", "k_norm_a_2", "sinks_a_2", "lower_bounds_2", "g_norm_b_2", "w_out_even_2", "ln_odd_2",
        "w_in_odd_2", "w_out_odd_2")


def kernel(**inputs):
    import concourse.bacc as bacc
    from concourse.bass_utils import run_bass_kernel_spmd

    nc = bacc.Bacc("TRN2", target_bir_lowering=False, num_devices=1)
    const_a, const_b = constants()
    arrays = {name: np.ascontiguousarray(inputs[name]) for name in _INS}
    arrays["const_a"], arrays["const_b"] = const_a, const_b
    ins = {name: nc.dram_tensor(f"in_{name}", a.shape, mybir.dt.from_np(a.dtype), kind="ExternalInput").ap()
           for name, a in arrays.items()}
    out = nc.dram_tensor("out_x", (1, SEQ, D), F32, kind="ExternalOutput").ap()
    two_blocks_kernel(nc, ins, out)
    r = run_bass_kernel_spmd(nc, [{f"in_{name}": a for name, a in arrays.items()}], core_ids=[0])
    return r.results[0]["out_x"]
```
